# Optimizing a Trainium2 kernel written in Bass

```python
import jax, jax.numpy as jnp
from jax import lax
import numpy as np

D_MODEL = 1024
BATCH = 1
SEQ = 256
DEPTH = 2

HEAD_DIM = 64
N_Q_A = 16
N_KV_A = 2
GROUP_A = N_Q_A // N_KV_A
WINDOW = 128
BLOCK = 128
N_H_B = 16
ROT_DIM = HEAD_DIM // 4
ROPE_THETA = 500000.0
D_FF = -(-8 * D_MODEL // (3 * 256)) * 256
N_MIXERS = 2
N_A = (DEPTH + 1) // 2
N_B = DEPTH // 2
QKV_A = (N_Q_A + 2 * N_KV_A) * HEAD_DIM
QKV_B = 3 * N_H_B * HEAD_DIM
EPS = 1e-6


def rmsnorm(x, gain):
    xf = x.astype(jnp.float32)
    y = xf * lax.rsqrt(jnp.mean(xf * xf, axis=-1, keepdims=True) + EPS)
    return (y * gain.astype(jnp.float32)).astype(x.dtype)

def partial_rope(x, positions):
    half = ROT_DIM // 2
    inv_freq = jnp.power(jnp.float32(ROPE_THETA), -jnp.arange(half, dtype=jnp.float32) * 2.0 / ROT_DIM)
    ang = positions.astype(jnp.float32)[:, :, None, None] * inv_freq
    cos, sin = jnp.cos(ang), jnp.sin(ang)
    xr = x[..., :ROT_DIM].astype(jnp.float32)
    x1, x2 = xr[..., :half], xr[..., half:]
    rot = jnp.concatenate([x1 * cos - x2 * sin, x2 * cos + x1 * sin], axis=-1).astype(x.dtype)
    return jnp.concatenate([rot, x[..., ROT_DIM:]], axis=-1)

def sliding_window_sink_attention(h, positions, w_qkv, q_gain, k_gain, sinks, w_o):
    B, S, _ = h.shape
    qkv = h @ w_qkv
    q, k, v = jnp.split(qkv, [N_Q_A * HEAD_DIM, (N_Q_A + N_KV_A) * HEAD_DIM], axis=-1)
    q = q.reshape(B, S, N_Q_A, HEAD_DIM)
    k = k.reshape(B, S, N_KV_A, HEAD_DIM)
    v = v.reshape(B, S, N_KV_A, HEAD_DIM)
    q = partial_rope(rmsnorm(q, q_gain), positions)
    k = partial_rope(rmsnorm(k, k_gain), positions)
    q = q.reshape(B, S, N_KV_A, GROUP_A, HEAD_DIM)
    pad = jnp.zeros((B, BLOCK, N_KV_A, HEAD_DIM), k.dtype)
    kp = jnp.concatenate([pad, k], axis=1)
    vp = jnp.concatenate([pad, v], axis=1)
    scale = HEAD_DIM ** -0.5
    q_idx = jnp.arange(BLOCK)[:, None] + BLOCK
    k_idx = jnp.arange(2 * BLOCK)[None, :]
    rel = q_idx - k_idx
    band = (rel >= 0) & (rel < WINDOW)
    sink_logit = sinks.astype(jnp.float32).reshape(1, N_KV_A, GROUP_A, 1, 1)

    def block_fn(i):
        start = i * BLOCK
        qb = lax.dynamic_slice_in_dim(q, start, BLOCK, axis=1)
        kb = lax.dynamic_slice_in_dim(kp, start, 2 * BLOCK, axis=1)
        vb = lax.dynamic_slice_in_dim(vp, start, 2 * BLOCK, axis=1)
        s = jnp.einsum('bqkgd,bskd->bkgqs', qb, kb).astype(jnp.float32) * scale
        valid = band & (start - BLOCK + k_idx >= 0)
        s = jnp.where(valid, s, -jnp.inf)
        sink_col = jnp.broadcast_to(sink_logit, s.shape[:-1] + (1,))
        p = jax.nn.softmax(jnp.concatenate([s, sink_col], axis=-1), axis=-1)[..., :-1]
        o = jnp.einsum('bkgqs,bskd->bqkgd', p.astype(vb.dtype), vb)
        return o.reshape(B, BLOCK, N_Q_A * HEAD_DIM)

    out = lax.map(block_fn, jnp.arange(S // BLOCK))
    out = jnp.moveaxis(out, 0, 1).reshape(B, S, N_Q_A * HEAD_DIM)
    return out @ w_o

def stick_breaking_attention(h, w_qkv, w_o):
    B, S, _ = h.shape
    qkv = h @ w_qkv
    q, k, v = jnp.split(qkv, 3, axis=-1)
    q = q.reshape(B, S, N_H_B, HEAD_DIM)
    k = k.reshape(B, S, N_H_B, HEAD_DIM)
    v = v.reshape(B, S, N_H_B, HEAD_DIM)
    scale = HEAD_DIM ** -0.5
    k_idx = jnp.arange(S)[None, :]

    def block_fn(i):
        start = i * BLOCK
        qb = lax.dynamic_slice_in_dim(q, start, BLOCK, axis=1)
        z = jnp.einsum('bqhd,bshd->bhqs', qb, k).astype(jnp.float32) * scale
        t_idx = start + jnp.arange(BLOCK)[:, None]
        strict = k_idx < t_idx
        log_beta = jax.nn.log_sigmoid(z)
        log_one_minus = jnp.where(strict, jax.nn.log_sigmoid(-z), 0.0)
        rc = lax.cumsum(log_one_minus, axis=3, reverse=True)
        after = jnp.pad(rc[..., 1:], ((0, 0), (0, 0), (0, 0), (0, 1)))
        a = jnp.where(strict, jnp.exp(log_beta + after), 0.0)
        o = jnp.einsum('bhqs,bshd->bqhd', a.astype(v.dtype), v)
        return o.reshape(B, BLOCK, N_H_B * HEAD_DIM)

    out = lax.map(block_fn, jnp.arange(S // BLOCK))
    out = jnp.moveaxis(out, 0, 1).reshape(B, S, N_H_B * HEAD_DIM)
    return out @ w_o

def swiglu(h, w_gate, w_up, w_down):
    return (jax.nn.silu(h @ w_gate) * (h @ w_up)) @ w_down

def first_inputs(seed: int = 0) -> dict:
    key = jax.random.key(seed)
    ks = jax.random.split(key, 20)
    f32 = jnp.float32
    nrm = lambda k, shape, s: jax.random.normal(k, shape, f32) * s
    x = jax.random.normal(ks[0], (BATCH, SEQ, D_MODEL), f32)
    c = jax.random.normal(ks[1], (BATCH, D_MODEL), f32)
    offset = jax.random.randint(ks[2], (BATCH, 1), 0, 4096, dtype=jnp.int32)
    positions = offset + jnp.arange(SEQ, dtype=jnp.int32)[None, :]
    return {
        'x': x,
        'c': c,
        'positions': positions,
        'ada_w': nrm(ks[3], (DEPTH, D_MODEL, 6 * D_MODEL), 0.5 * D_MODEL ** -0.5),
        'ada_b': nrm(ks[4], (DEPTH, 6 * D_MODEL), 0.01),
        'norm1_g': 1.0 + nrm(ks[5], (DEPTH, D_MODEL), 0.05),
        'norm2_g': 1.0 + nrm(ks[6], (DEPTH, D_MODEL), 0.05),
        'wqkv_a': nrm(ks[7], (N_A, D_MODEL, QKV_A), D_MODEL ** -0.5),
        'q_norm_a': 1.0 + nrm(ks[8], (N_A, HEAD_DIM), 0.05),
        'k_norm_a': 1.0 + nrm(ks[9], (N_A, HEAD_DIM), 0.05),
        'sinks_a': nrm(ks[10], (N_A, N_Q_A), 1.0),
        'wo_a': nrm(ks[11], (N_A, N_Q_A * HEAD_DIM, D_MODEL), (N_Q_A * HEAD_DIM) ** -0.5),
        'wqkv_b': nrm(ks[12], (N_B, D_MODEL, QKV_B), D_MODEL ** -0.5),
        'wo_b': nrm(ks[13], (N_B, N_H_B * HEAD_DIM, D_MODEL), (N_H_B * HEAD_DIM) ** -0.5),
        'w_gate': nrm(ks[14], (DEPTH, D_MODEL, D_FF), D_MODEL ** -0.5),
        'w_up': nrm(ks[15], (DEPTH, D_MODEL, D_FF), D_MODEL ** -0.5),
        'w_down': nrm(ks[16], (DEPTH, D_FF, D_MODEL), D_FF ** -0.5),
    }

def first_block(x, c, positions, ada_w, ada_b, norm1_g, norm2_g, wqkv_a, q_norm_a, k_norm_a,
              sinks_a, wo_a, wqkv_b, wo_b, w_gate, w_up, w_down):
    cond = jax.nn.silu(c)
    for i in range(DEPTH):
        mod = (cond @ ada_w[i] + ada_b[i])[:, None, :]
        sh1, sc1, g1, sh2, sc2, g2 = jnp.split(mod, 6, axis=-1)
        h = rmsnorm(x, norm1_g[i]) * (1.0 + sc1) + sh1
        j = i // N_MIXERS
        if i % N_MIXERS == 0:
            y = sliding_window_sink_attention(h, positions, wqkv_a[j], q_norm_a[j], k_norm_a[j],
                                              sinks_a[j], wo_a[j])
        else:
            y = stick_breaking_attention(h, wqkv_b[j], wo_b[j])
        x = x + g1 * y
        h = rmsnorm(x, norm2_g[i]) * (1.0 + sc2) + sh2
        x = x + g2 * swiglu(h, w_gate[i], w_up[i], w_down[i])
    return x


DEPTH_2 = 1

D_MIX = D_MODEL
D_A = D_MIX // 2
D_B = D_MIX - D_A
N_HEADS_A = 8
HEAD_DIM_A = D_A // N_HEADS_A
N_GROUPS_B = 8
GROUP_DIM_B = D_B // N_GROUPS_B
CHUNK = 128
CONV_WIDTH = 31
D_IN = 2 * D_A + 2 * D_B
D_FF_2 = -(-8 * D_MODEL // (3 * 256)) * 256
N_MOD = 6


def rmsnorm_2(x, g):
    xf = x.astype(jnp.float32)
    y = xf * lax.rsqrt(jnp.mean(xf * xf, axis=-1, keepdims=True) + EPS)
    return (y * g.astype(jnp.float32)).astype(x.dtype)

def layernorm(x, g, b):
    xf = x.astype(jnp.float32)
    mu = jnp.mean(xf, axis=-1, keepdims=True)
    xc = xf - mu
    var = jnp.mean(xc * xc, axis=-1, keepdims=True)
    y = xc * lax.rsqrt(var + EPS) * g.astype(jnp.float32) + b.astype(jnp.float32)
    return y.astype(x.dtype)

def modulate(h, shift, scale):
    return h * (1 + scale[:, None, :]) + shift[:, None, :]

def spatial_gating_mixer(u, v, ln_g, ln_b, w_s, b_s):
    B, S, _ = v.shape
    v = layernorm(v, ln_g, ln_b)
    v = v.reshape(B, S // CHUNK, CHUNK, N_HEADS_A, HEAD_DIM_A)
    causal = jnp.tril(jnp.ones((CHUNK, CHUNK), dtype=bool))
    w = jnp.where(causal[None], w_s, jnp.zeros_like(w_s)).astype(v.dtype)
    mixed = jnp.einsum('hts,bcshd->bcthd', w, v) + b_s.T.astype(v.dtype)[None, None, :, :, None]
    return u * mixed.reshape(B, S, D_A)

def conformer_conv_mixer(val, gate, conv_w, conv_b, gn_g, gn_b):
    B, S, _ = val.shape
    y = val * jax.nn.sigmoid(gate)
    y = lax.conv_general_dilated(
        y, conv_w[:, None, :].astype(y.dtype), window_strides=(1,),
        padding=[(CONV_WIDTH - 1, 0)],
        dimension_numbers=('NWC', 'WIO', 'NWC'),
        feature_group_count=D_B) + conv_b.astype(y.dtype)
    y = y.reshape(B, S, N_GROUPS_B, GROUP_DIM_B)
    y = layernorm(y, gn_g.reshape(N_GROUPS_B, GROUP_DIM_B), gn_b.reshape(N_GROUPS_B, GROUP_DIM_B))
    return jax.nn.silu(y.reshape(B, S, D_B))

def second_inputs(seed: int = 0) -> dict:
    key = jax.random.key(seed)
    ks = jax.random.split(key, 24)
    f32 = jnp.float32
    nrm = lambda k, shape, s: jax.random.normal(k, shape, f32) * s
    L = DEPTH_2
    return {
        "x": jax.random.normal(ks[0], (BATCH, SEQ, D_MODEL), f32),
        "c": jax.random.normal(ks[1], (BATCH, D_MODEL), f32),
        "ada_w": nrm(ks[2], (L, D_MODEL, N_MOD * D_MODEL), D_MODEL ** -0.5),
        "ada_b": nrm(ks[3], (L, N_MOD * D_MODEL), 0.02),
        "norm1_g": 1.0 + nrm(ks[4], (L, D_MODEL), 0.05),
        "w_in": nrm(ks[5], (L, D_MODEL, D_IN), D_MODEL ** -0.5),
        "b_in": nrm(ks[6], (L, D_IN), 0.02),
        "a_ln_g": 1.0 + nrm(ks[7], (L, D_A), 0.05),
        "a_ln_b": nrm(ks[8], (L, D_A), 0.02),
        "a_spatial_w": nrm(ks[9], (L, N_HEADS_A, CHUNK, CHUNK), CHUNK ** -0.5),
        "a_spatial_b": 1.0 + nrm(ks[10], (L, N_HEADS_A, CHUNK), 0.1),
        "b_conv_w": nrm(ks[11], (L, CONV_WIDTH, D_B), CONV_WIDTH ** -0.5),
        "b_conv_b": nrm(ks[12], (L, D_B), 0.02),
        "b_gn_g": 1.0 + nrm(ks[13], (L, D_B), 0.05),
        "b_gn_b": nrm(ks[14], (L, D_B), 0.02),
        "out_norm_a_g": 1.0 + nrm(ks[15], (L, D_A), 0.05),
        "out_norm_b_g": 1.0 + nrm(ks[16], (L, D_B), 0.05),
        "w_out": nrm(ks[17], (L, D_MIX, D_MODEL), D_MIX ** -0.5),
        "norm2_g": 1.0 + nrm(ks[18], (L, D_MODEL), 0.05),
        "w_ffn_in": nrm(ks[19], (L, D_MODEL, 2 * D_FF_2), D_MODEL ** -0.5),
        "w_ffn_out": nrm(ks[20], (L, D_FF_2, D_MODEL), D_FF_2 ** -0.5),
        "ada_f_w": nrm(ks[21], (D_MODEL, 2 * D_MODEL), D_MODEL ** -0.5),
        "ada_f_b": nrm(ks[22], (2 * D_MODEL,), 0.02),
        "norm_f_g": 1.0 + nrm(ks[23], (D_MODEL,), 0.05),
    }

def second_block(x, c, ada_w, ada_b, norm1_g, w_in, b_in, a_ln_g, a_ln_b, a_spatial_w,
              a_spatial_b, b_conv_w, b_conv_b, b_gn_g, b_gn_b, out_norm_a_g, out_norm_b_g,
              w_out, norm2_g, w_ffn_in, w_ffn_out, ada_f_w, ada_f_b, norm_f_g):
    c_act = jax.nn.silu(c)
    for i in range(DEPTH_2):
        cond = c_act @ ada_w[i] + ada_b[i]
        shift1, scale1, gate1, shift2, scale2, gate2 = jnp.split(cond, N_MOD, axis=-1)

        h = modulate(rmsnorm_2(x, norm1_g[i]), shift1, scale1)
        z = h @ w_in[i] + b_in[i]
        u, v, val, gate = jnp.split(z, [D_A, 2 * D_A, 2 * D_A + D_B], axis=-1)
        y_a = spatial_gating_mixer(jax.nn.gelu(u, approximate=False),
                                   jax.nn.gelu(v, approximate=False),
                                   a_ln_g[i], a_ln_b[i], a_spatial_w[i], a_spatial_b[i])
        y_b = conformer_conv_mixer(val, gate, b_conv_w[i], b_conv_b[i], b_gn_g[i], b_gn_b[i])
        y = jnp.concatenate([rmsnorm_2(y_a, out_norm_a_g[i]), rmsnorm_2(y_b, out_norm_b_g[i])], axis=-1)
        x = x + gate1[:, None, :] * (y @ w_out[i])

        h2 = modulate(rmsnorm_2(x, norm2_g[i]), shift2, scale2)
        g_ff, up_ff = jnp.split(h2 @ w_ffn_in[i], 2, axis=-1)
        x = x + gate2[:, None, :] * ((jax.nn.silu(g_ff) * up_ff) @ w_ffn_out[i])

    shift_f, scale_f = jnp.split(c_act @ ada_f_w + ada_f_b, 2, axis=-1)
    return modulate(rmsnorm_2(x, norm_f_g), shift_f, scale_f)


def setup_inputs(seed=0):
    out = dict(first_inputs(seed))
    for name, value in second_inputs(seed + 1).items():
        if name != "x":
            out[name + "_2"] = value
    return out


def reference(
    x, c, positions, ada_w, ada_b, norm1_g, norm2_g, wqkv_a, q_norm_a, k_norm_a, sinks_a, wo_a,
    wqkv_b, wo_b, w_gate, w_up, w_down, c_2, ada_w_2, ada_b_2, norm1_g_2, w_in_2, b_in_2,
    a_ln_g_2, a_ln_b_2, a_spatial_w_2, a_spatial_b_2, b_conv_w_2, b_conv_b_2, b_gn_g_2,
    b_gn_b_2, out_norm_a_g_2, out_norm_b_g_2, w_out_2, norm2_g_2, w_ffn_in_2, w_ffn_out_2,
    ada_f_w_2, ada_f_b_2, norm_f_g_2,
):
    x = first_block(
        x, c, positions, ada_w, ada_b, norm1_g, norm2_g, wqkv_a, q_norm_a, k_norm_a, sinks_a,
        wo_a, wqkv_b, wo_b, w_gate, w_up, w_down,
    )
    return second_block(
        x, c_2, ada_w_2, ada_b_2, norm1_g_2, w_in_2, b_in_2, a_ln_g_2, a_ln_b_2, a_spatial_w_2,
        a_spatial_b_2, b_conv_w_2, b_conv_b_2, b_gn_g_2, b_gn_b_2, out_norm_a_g_2,
        out_norm_b_g_2, w_out_2, norm2_g_2, w_ffn_in_2, w_ffn_out_2, ada_f_w_2, ada_f_b_2,
        norm_f_g_2,
    )


_drawn_inputs = setup_inputs


def setup_inputs(seed=0):
    import zlib

    import numpy as np

    out = dict(_drawn_inputs(seed))
    spreads = {}
    factors = {'ada_b': 3.793,
     'norm1_g': 4.121,
     'q_norm_a': 8.0,
     'k_norm_a': 8.0,
     'sinks_a': 6.178,
     'b_in_2': 6.057,
     'a_ln_g_2': 18.811,
     'a_ln_b_2': 43.473,
     'b_conv_b_2': 4.953,
     'b_gn_g_2': 7.866,
     'b_gn_b_2': 40.211,
     'out_norm_a_g_2': 3.547,
     'out_norm_b_g_2': 2.994,
     'a_spatial_b_2': 4.201,
     'norm2_g_2': 4.137,
     'ada_f_b_2': 2.717}
    for name, (base, spread) in spreads.items():
        noise = np.random.default_rng([zlib.crc32(name.encode()), seed]).standard_normal(out[name].shape)
        drawn = base * np.exp(spread * noise) if base else spread * noise
        out[name] = __import__('jax').numpy.asarray(drawn.astype(out[name].dtype))
    for name, factor in factors.items():
        out[name] = (out[name] * factor).astype(out[name].dtype)
    return out
```

```python
from contextlib import ExitStack

import numpy as np
import concourse.bass as bass
from concourse import mybir

F32 = mybir.dt.float32
F32R = mybir.dt.float32r
BF16 = mybir.dt.bfloat16
I32 = mybir.dt.int32
ALU = mybir.AluOpType
ACT = mybir.ActivationFunctionType
AX_X = mybir.AxisListType.X

P = 128
D = 1024
T = 256
KT = D // P
HD = 64
DFF = 2816
FT = DFF // P
FG = FT // 2
DA = 512
CONV = 31
EPS = 1e-6
THETA = 500000.0
ROT = HD // 4
SCALE = HD ** -0.5
NEG = -1e30

UNITS = [("qkv_a", 5), ("wo_a", 4), ("gu0", 22), ("dn0", 11), ("qkv_b", 12), ("wo_b", 4), ("gu1", 22),
         ("dn1", 11), ("w_in", 8), ("w_out", 4), ("gu2", 22), ("dn2", 11)]
BANKS = [("qkv_a", 2), ("wo_a", 2), ("gu0", 11), ("dn0", 6), ("qkv_b", 6), ("wo_b", 2), ("gu1", 11),
         ("dn1", 6), ("w_in", 4), ("w_out", 2), ("gu2", 11), ("dn2", 6)]


def starts(counts):
    at, out = 0, {}
    for name, n in counts:
        out[name] = at
        at += n
    return out


U0 = starts(UNITS)
BD = starts(BANKS)

FIRST_IDS = [0, 1, 2, 3]
ATTN_A_IDS = [4, 5, 6, 7, 8, 9]
GU_BLOCKS = [(10, 12, range(0, 6)), (22, 24, range(0, 6)), (34, 36, range(1, 5))]
DN_BLOCKS = [(16, 10), (28, 22), (38, 34)]
ATTN_B_BLOCKS = [(18, 18), (19, 19), (20, 20), (21, 21)]
MIX_BLOCKS = [(30, 30), (31, 31), (32, 32), (33, 33)]

ROWS = [("ada_b", 96), ("ada_b_2", 48), ("ada_f_b", 16), ("norm1_g", 16), ("norm2_g", 16), ("norm1_g_2", 8),
        ("norm2_g_2", 8), ("norm_f_g", 8), ("b_in_2", 16), ("b_conv_b_2", 4), ("b_gn_g_2", 4),
        ("b_gn_b_2", 4), ("out_norm_a_g_2", 4), ("out_norm_b_g_2", 4), ("q_norm_a", 1), ("k_norm_a", 1),
        ("b_conv_w_2", 4 * CONV)]
COL = starts(ROWS)
N_ROWS = sum(n for _, n in ROWS)
ROW_TILES = -(-N_ROWS // P)


def row_pieces():
    out = []
    for name, n in ROWS:
        r = 0
        while r < n:
            at = COL[name] + r
            k = min(n - r, P - at % P)
            out.append((name, r, k, at // P, at % P))
            r += k
    return out


KEPT = [("ident", P), ("rot", P), ("blk", P), ("ones", P), ("tneg", P), ("oneg", P), ("cols", 8)]
TEMP = [("swap", P), ("mask_a", 3 * P), ("mask_b", P)]
K0 = starts(KEPT)
K_W = sum(n for _, n in KEPT)
T0 = starts(TEMP)
T_W = sum(n for _, n in TEMP)
C_INVF, C_ROPE, C_KEEP, C_EPS, C_HALFPI, C_ONE = range(6)


def constants():
    k = np.zeros((P, K_W), np.float32)
    t = np.zeros((P, T_W), np.float32)
    tril = np.tril(np.ones((P, P), np.float32))
    i, j = np.arange(P)[:, None], np.arange(P)[None, :]
    k[:, K0["ident"]:K0["ident"] + P] = np.eye(P)
    half = ROT // 2
    rot = np.zeros((P, P), np.float32)
    for base in (0, HD):
        for d in range(half):
            rot[base + d + half, base + d] = -1.0
            rot[base + d, base + d + half] = 1.0
    k[:, K0["rot"]:K0["rot"] + P] = rot
    k[:, K0["blk"]:K0["blk"] + P] = (i // HD == j // HD) / HD
    k[:, K0["ones"]:K0["ones"] + P] = 1.0 / D
    k[:, K0["tneg"]:K0["tneg"] + P] = -(i >= j).astype(np.float32)
    k[:, K0["oneg"]:K0["oneg"] + P] = -1.0
    inv = np.power(np.float32(THETA), -np.arange(half, dtype=np.float32) * np.float32(2.0) / np.float32(ROT))
    c = k[:, K0["cols"]:]
    for base in (0, HD):
        c[base:base + half, C_INVF] = inv
        c[base + half:base + ROT, C_INVF] = inv
        c[base:base + ROT, C_ROPE] = 1.0
    c[:, C_KEEP] = 1.0 - c[:, C_ROPE]
    c[:, C_EPS] = EPS
    c[:, C_HALFPI] = np.pi / 2
    c[:, C_ONE] = 1.0
    t[:, T0["swap"]:T0["swap"] + P] = (i == (j + HD) % P)
    causal = np.where(j > i, NEG, 0.0)
    window = np.where(j <= i, NEG, 0.0)
    t[:, T0["mask_a"]:T0["mask_a"] + 3 * P] = np.concatenate([causal, window, causal], 1)
    t[:, T0["mask_b"]:T0["mask_b"] + P] = np.where(i >= j, NEG, 0.0)
    return k, t, tril


def two_pi_parts():
    parts, left = [], 2 * np.pi
    for bits in (6, 15, 24):
        q = np.floor(left * 2.0 ** bits) / 2.0 ** bits
        parts.append(float(q))
        left -= q
    parts.append(float(np.float32(left)))
    return parts


ROW_DMAS = len(row_pieces()) + 2

ROUND = 1.5 * 2.0 ** 23


def build(nc, a, out):
    ctx = ExitStack()
    with ctx:
        def sb(name, shape, dt=F32, stack=ctx):
            return stack.enter_context(nc.sbuf_tensor(name, shape, dt))

        def ps(name, shape):
            return ctx.enter_context(nc.psum_tensor(name, shape, F32))

        def sem(name):
            return ctx.enter_context(nc.semaphore(name))

        RAW = sb("RAW", [P, 4, 2048])
        WH = sb("WH", [P, 4, 2048], F32R)
        WL = sb("WL", [P, 4, 2048], F32R)
        ADA = sb("ADA", [P, 2, 4, 512])
        ACC = sb("ACC", [P, 2, 512])
        X = sb("X", [P, KT, T])
        XH = sb("XH", [P, KT, T], F32R)
        XL = sb("XL", [P, KT, T], F32R)
        TMP = sb("TMP", [P, KT, T])
        CONST = sb("CONST", [P, K_W])
        VC = sb("VC", [P, N_ROWS])
        MOD = sb("MOD", [P, 160])
        COND = sb("COND", [P, 2 * KT])
        COEF = sb("COEF", [P, KT])
        STD = sb("STD", [P, T])
        RSTD = sb("RSTD", [P, T])
        IDB = sb("IDB", [P, P], BF16)
        MASKA = sb("MASKA", [P, 3 * P], BF16)
        MASKB = sb("MASKB", [P, P], BF16)

        s1 = ExitStack()
        with s1:
            VROWS = sb("VROWS", [P, ROW_TILES, P], F32, s1)
            CROWS = sb("CROWS", [2 * KT, P], F32, s1)
            CTMP = sb("CTMP", [P, T_W], F32, s1)
            POSI = sb("POSI", [P, T], I32, s1)
            ANG = sb("ANG", [P, 4, T], F32, s1)
            COS = sb("COS", [P, T], F32, s1)
            SIN = sb("SIN", [P, T], F32, s1)
            SINK = sb("SINK", [P, 2, 16], F32, s1)
            NSINK = sb("NSINK", [P, 2, 16], F32, s1)
            QA = sb("QA", [P, 9, T], F32, s1)
            KS = sb("KS", [P, T], F32, s1)
            VA = sb("VA", [P, 2, P], F32, s1)
            QSQ = sb("QSQ", [P, 2, T], F32, s1)
            QSTD = sb("QSTD", [P, 2, T], F32, s1)
            QRS = sb("QRS", [P, 2, T], F32, s1)
            QN = sb("QN", [P, 2, T], F32, s1)
            QT2 = sb("QT2", [P, 2, T], F32, s1)
            PR = sb("PR", [P, 2, 2, 384], F32, s1)
            PT = sb("PT", [P, 2, 2, 384], F32, s1)
            SM = sb("SM", [P, 2, 6, 4], F32, s1)
            RS_SUM = sb("RS_SUM", [P, 2, 4], F32, s1)
        s2 = ExitStack()
        with s2:
            QB = sb("QB", [P, KT, T], F32, s2)
            KB = sb("KB", [P, KT, T], F32, s2)
            VB = sb("VB", [P, 2, D], F32, s2)
            ZP = sb("ZP", [P, 2, 384], F32, s2)
            AZ = sb("AZ", [P, 2, 384], F32, s2)
            EX = sb("EX", [P, 2, 384], F32, s2)
            LN = sb("LN", [P, 2, 384], F32, s2)
            SP = sb("SP", [P, 2, 384], F32, s2)
            AB = sb("AB", [P, 2, 384], F32, s2)
        s3 = ExitStack()
        with s3:
            WSP = sb("WSP", [P, 8, P], F32, s3)
            TRIL = sb("TRIL", [P, P], F32, s3)
            WT = sb("WT", [P, 8, P], F32, s3)
            BSB = sb("BSB", [P, 4, P], F32, s3)
            LNG = sb("LNG", [P, DA], F32, s3)
            LNB = sb("LNB", [P, DA], F32, s3)
            BV = sb("BV", [P, DA], F32, s3)
            SG = sb("SG", [P, 4, T], F32, s3)
            Y0 = sb("Y0", [P, 4, CONV - 1 + T], F32, s3)
            CV = sb("CV", [P, 4, T], F32, s3)
            UG = sb("UG", [P, 4, T], F32, s3)
            VX = sb("VX", [P, 2, DA], F32, s3)
            VN = sb("VN", [P, 2, DA], F32, s3)
            VST = sb("VST", [P, 2, 8], F32, s3)
        s4 = ExitStack()
        with s4:
            XO = sb("XO", [P, KT, T], F32, s4)
            OUT = sb("OUT", [P, 2, D], F32, s4)
        MH = sb("MH", [P, FT, T], F32R)
        ML = sb("ML", [P, FT, T], F32R)
        MHF, MLF = (m[:, :, :].rearrange("p f t -> p (f t)") for m in (MH, ML))

        M = ps("M", [P, 8, T])
        AUX = ps("AUX", [P, 8, T])
        MB = M[:, :, :].rearrange("p (b h) t -> p b (h t)", h=2)
        AB4 = AUX[:, :, :].rearrange("p (b h) t -> p b (h t)", h=2)
        ADP = AUX[:, 6, 0:4]

        def kc(name, n=P):
            return CONST[:, K0[name]:K0[name] + n]

        def cc(i):
            return CONST[:, K0["cols"] + i:K0["cols"] + i + 1]

        def vc(name, i, n=1):
            return VC[:, COL[name] + i:COL[name] + i + n]

        def mod(layer, chunk, i, n=1):
            at = layer * 48 + chunk * 8 + i
            return MOD[:, at:at + n]

        IDENT, ROTM, BLK, ONES, TNEG, ONEG = (kc(n) for n in ("ident", "rot", "blk", "ones", "tneg", "oneg"))
        XTOK = TMP[:, :, :].rearrange("p (m a) t -> p m (a t)", m=2)

        landed = [sem(f"landed{i}") for i in range(4)]
        h_ready, l_ready, w_used, bank_done = sem("h_ready"), sem("l_ready"), sem("w_used"), sem("bank_done")
        a_landed = [sem(f"a_landed{i}") for i in range(2)]
        a_chain, acc_red, mod_ready = sem("a_chain"), sem("acc_red"), sem("mod_ready")
        x_ready, sq_ready, ssq_ready, std_ready = sem("x_ready"), sem("sq_ready"), sem("ssq_ready"), sem("std_ready")
        rstd_ready, coef_ready, t_ready = sem("rstd_ready"), sem("coef_ready"), sem("t_ready")
        hh_ready, xin_ready = sem("hh_ready"), sem("xin_ready")
        silu_ready, midf_ready, midh_ready, mid_ready = (sem(n) for n in ("silu_ready", "midf_ready", "midh_ready", "mid_ready"))
        crows_in, const_in, rows_in, x_in, misc_in = (sem(n) for n in ("crows_in", "const_in", "rows_in", "x_in", "misc_in"))
        c_turned, cond_ready, rows_turned, vc_ready, x_turned = (sem(n) for n in ("c_turned", "cond_ready", "rows_turned", "vc_ready", "x_turned"))
        masks_ready, ang_v, ang_s, trig_ready, sink_ready, gain_ready = (
            sem(n) for n in ("masks_ready", "ang_v", "ang_s", "trig_ready", "sink_ready", "gain_ready"))
        qa_sq, qa_ssq, qa_std, qa_rs, qa_n, qa_rot, qa_c, qa_t2, qa_q, ks_t, ks_ready, va_ready = (
            sem(n) for n in ("qa_sq", "qa_ssq", "qa_std", "qa_rs", "qa_n", "qa_rot", "qa_c", "qa_t2", "qa_q", "ks_t", "ks_ready", "va_ready"))
        sa_s, sa_m, sa_nm, sa_d, sa_p, sa_e, sa_t, sa_r, sa_pn, sa_tr, sa_ptc, sa_o = (
            sem(n) for n in ("sa_s", "sa_m", "sa_nm", "sa_d", "sa_p", "sa_e", "sa_t", "sa_r", "sa_pn", "sa_tr", "sa_ptc", "sa_o"))
        qb_ev, sb_z, sb_zp, sb_az, sb_ex, sb_ln, sb_sp, sb_e, sb_a, sb_o = (
            sem(n) for n in ("qb_ev", "sb_z", "sb_zp", "sb_az", "sb_ex", "sb_ln", "sb_sp", "sb_e", "sb_a", "sb_o"))
        mx_in, mx_tril, mx_wt_t, mx_wt, mx_pad, mx_sg, mx_y0, cv_c, ug_ready = (
            sem(n) for n in ("mx_in", "mx_tril", "mx_wt_t", "mx_wt", "mx_pad", "mx_sg", "mx_y0", "cv_c", "ug_ready"))
        v_x, v_g, v_mu, v_c, v_s2, v_sd, v_rs, v_n, v_b = (sem(n) for n in ("v_x", "v_g", "v_mu", "v_c", "v_s2", "v_sd", "v_rs", "v_n", "v_b"))
        gn_mu, gn_c, gn_sq, gn_var, gn_std, gn_rs, gn_n, yb_ready = (
            sem(n) for n in ("gn_mu", "gn_c", "gn_sq", "gn_var", "gn_std", "gn_rs", "gn_n", "yb_ready"))
        sp_done, ya_t, ya_ready = sem("sp_done"), sem("ya_t"), sem("ya_ready")
        on_sq, on_ssq, on_std, on_rs, on_t = (sem(n) for n in ("on_sq", "on_ssq", "on_std", "on_rs", "on_t"))
        xo_ready, o_turned, o_copied, o_stored = (sem(n) for n in ("xo_ready", "o_turned", "o_copied", "o_stored"))

        def kp(w):
            return w.rearrange("(t p) n -> p t n", p=P)

        ada_src = [kp(a["ada_w"][0]), kp(a["ada_w"][1]), kp(a["ada_w_2"][0]), kp(a["ada_f_w"])]
        gate_src = [kp(a["w_gate"][0]), kp(a["w_gate"][1]), kp(a["w_ffn_in_2"][0])[:, :, 0:DFF]]
        up_src = [kp(a["w_up"][0]), kp(a["w_up"][1]), kp(a["w_ffn_in_2"][0])[:, :, DFF:2 * DFF]]
        down_src = [kp(a["w_down"][0]), kp(a["w_down"][1]), kp(a["w_ffn_out_2"][0])]
        qkv_a_src, wo_a_src = kp(a["wqkv_a"][0]), kp(a["wo_a"][0])
        qkv_b_src, wo_b_src = kp(a["wqkv_b"][0]), kp(a["wo_b"][0])
        in_src, out_src = kp(a["w_in_2"][0]), kp(a["w_out_2"][0])
        IN_COLS = [3 * DA, 2 * DA, DA, 0]

        def slot(base, k):
            return (base + k) % 4

        def landed_by(base, k, i):
            return 32 * ((base + k) // 4 + 1) + 32 * i

        block = ctx.enter_context(nc.Block())

        @block.sync
        def _(sp):
            sp.dma_start(CROWS[0:KT, :], a["c"].rearrange("a (t p) -> (a t) p", p=P)).then_inc(crows_in, 16)
            sp.dma_start(CROWS[KT:2 * KT, :], a["c_2"].rearrange("a (t p) -> (a t) p", p=P)).then_inc(crows_in, 16)

            def ada_load(src, col, b, i=0):
                if not isinstance(col, int):
                    col = sp.snap(col)
                for h in range(2):
                    if b > 0:
                        sp.wait_ge(a_chain, 8 * b + 4 * h - 4 + 8 * i)
                    sp.dma_start(ADA[:, h, :, :], src[:, 4 * h:4 * h + 4, bass.ds(col, 512)]).then_inc(a_landed[h], 16)

            def ada_by_id(b, ident):
                ada_load(ada_src[ident // 12], 512 * (ident % 12), b)

            def unit_free(base, k, i=0):
                if base + k >= 4:
                    sp.wait_ge(l_ready, base + k - 3 + 4 * i)

            def load_square(base, k, src, col):
                unit_free(base, k)
                s, t0 = slot(base, k), 4 * (k % 2)
                for q in range(2):
                    sp.dma_start(RAW[:, s, 1024 * q:1024 * q + 1024].rearrange("p (t n) -> p t n", t=2),
                                 src[:, t0 + 2 * q:t0 + 2 * q + 2, col:col + 512]).then_inc(landed[s], 16)

            def load_gate_up(layer, base, k, col, i=0):
                unit_free(base, k, i)
                s, t0 = slot(base, k), 4 * (k % 2)
                view = RAW[:, s, :].rearrange("p (t n) -> p t n", t=4)
                sp.dma_start(view[:, :, 0:256], gate_src[layer][:, t0:t0 + 4, bass.ds(col, 256)]).then_inc(landed[s], 16)
                sp.dma_start(view[:, :, 256:512], up_src[layer][:, t0:t0 + 4, bass.ds(col, 256)]).then_inc(landed[s], 16)

            def load_down(layer, base, k, row, i=0):
                rows = [row, row + 1]
                unit_free(base, k, i)
                s = slot(base, k)
                for q in range(2):
                    sp.dma_start(RAW[:, s, 1024 * q:1024 * q + 1024].rearrange("p (t n) -> p t n", t=1),
                                 down_src[layer][:, bass.ds(rows[q], 1), :]).then_inc(landed[s], 16)

            def feed_forward(layer):
                base, (b0, id0, steps) = U0[f"gu{layer}"], GU_BLOCKS[layer]
                col0 = 512 * (id0 % 12)
                src = ada_src[id0 // 12]

                def step(i, n_units, blk, first=0, before=0):
                    if blk:
                        nth = i + (before - first)
                        ada_load(src, nth * 512 + col0, b0, nth)
                    for k in range(n_units):
                        load_gate_up(layer, base + 4 * before, k, i * 512 + (512 * before + 256 * (k // 2)), i)

                step(0, 4, 0 in steps)
                with sp.Fori(0, 4) as i:
                    step(i, 4, True, steps[0], before=1)
                step(5, 2, 5 in steps)
                base, (b0, id0) = U0[f"dn{layer}"], DN_BLOCKS[layer]
                for k in range(3):
                    load_down(layer, base, k, 2 * k)
                with sp.Fori(0, 2) as i:
                    ada_load(ada_src[id0 // 12], i * 512 + 512 * (id0 % 12), b0, i)
                    for k in range(3, 7):
                        load_down(layer, base, k, i * 8 + 2 * k, i)

            for b, ident in enumerate(FIRST_IDS):
                ada_by_id(b, ident)
                if b == 0:
                    sp.dma_start(XTOK, a["x"][0].rearrange("(m p) d -> p m d", p=P)).then_inc(x_in, 16)
            for g in range(2):
                for k in range(2):
                    load_square(U0["qkv_a"], 2 * g + k, qkv_a_src, 512 * g)
            ada_by_id(4, 4)
            unit_free(U0["qkv_a"], 4)
            for q in range(2):
                sp.dma_start(RAW[:, 0, 1024 * q:1024 * q + 1024].rearrange("p (t n) -> p t n", t=4),
                             qkv_a_src[:, 4 * q:4 * q + 4, D:D + 256]).then_inc(landed[0], 16)
            ada_by_id(5, 5)
            for k in range(4):
                load_square(U0["wo_a"], k, wo_a_src, 512 * (k // 2))
            for b in range(6, 10):
                ada_by_id(b, ATTN_A_IDS[b - 4])
            feed_forward(0)

            for g in range(6):
                if g in (1, 4, 5):
                    ada_by_id(*ATTN_B_BLOCKS[(1, 4, 5).index(g)])
                for k in range(2):
                    load_square(U0["qkv_b"], 2 * g + k, qkv_b_src, 512 * g)
            ada_by_id(*ATTN_B_BLOCKS[3])
            for k in range(4):
                load_square(U0["wo_b"], k, wo_b_src, 512 * (k // 2))
            feed_forward(1)

            for g in range(4):
                if g == 1:
                    ada_by_id(*MIX_BLOCKS[0])
                for k in range(2):
                    load_square(U0["w_in"], 2 * g + k, in_src, IN_COLS[g])
            ada_by_id(*MIX_BLOCKS[1])
            for k in range(4):
                if k == 2:
                    ada_by_id(*MIX_BLOCKS[2])
                load_square(U0["w_out"], k, out_src, 512 * (k // 2))
            ada_by_id(*MIX_BLOCKS[3])
            feed_forward(2)

            for m in range(2):
                sp.wait_ge(o_copied, 2 * m + 2)
                sp.dma_start(out[0, m * P:(m + 1) * P, :], OUT[:, m, :]).then_inc(o_stored, 16)
            sp.wait_ge(o_stored, 32)

        @block.gpsimd
        def _(pool):
            pool.wait_ge(w_used, U0["w_in"])
            pool.dma_start(WSP[:, :, :], a["a_spatial_w_2"][0].rearrange("h t s -> t h s")).then_inc(mx_in, 16)
            pool.dma_start(TRIL[:, :], a["tril"]).then_inc(mx_in, 16)
            for e in range(2):
                pool.dma_start(BSB[HD * e:HD * e + HD, :, :],
                               a["a_spatial_b_2"][0].rearrange("(j e) t -> e j t", e=2)[e].partition_broadcast(HD)).then_inc(mx_in, 16)
            pool.dma_start(LNG[:, :], a["a_ln_g_2"][0].partition_broadcast(P)).then_inc(mx_in, 16)
            pool.dma_start(LNB[:, :], a["a_ln_b_2"][0].partition_broadcast(P)).then_inc(mx_in, 16)
            pool.dma_start(BV[:, :], a["b_in_2"][0, DA:2 * DA].partition_broadcast(P)).then_inc(mx_in, 16)

        @block.scalar
        def _(act):
            act.dma_start(CONST[:, :], a["kept"]).then_inc(const_in, 16)
            act.dma_start(CTMP[:, :], a["temp"]).then_inc(misc_in, 16)
            act.dma_start(POSI[:, :], a["positions"][0].partition_broadcast(P)).then_inc(misc_in, 16)
            for h in range(2):
                act.dma_start(SINK[:, h, :], a["sinks_a"][0].partition_broadcast(P)).then_inc(misc_in, 16)
            for name, r, n, tile, at in row_pieces():
                src = a[name]
                if name in ("q_norm_a", "k_norm_a"):
                    for h in range(2):
                        act.dma_start(VROWS[at:at + 1, tile, HD * h:HD * h + HD], src).then_inc(rows_in, 16)
                    continue
                if name == "ada_f_b" or name == "norm_f_g":
                    view = src.rearrange("(t p) -> t p", p=P)
                elif name == "b_conv_w_2":
                    view = src[0].rearrange("k (j p) -> (k j) p", p=P)
                else:
                    view = src.rearrange("l (t p) -> (l t) p", p=P)
                act.dma_start(VROWS[at:at + n, tile, :], view[r:r + n, :]).then_inc(rows_in, 16)

            def high(base, k, i=0):
                s = slot(base, k)
                act.wait_ge(landed[s], landed_by(base, k, i))
                if base + k >= 4:
                    act.wait_ge(w_used, base + k - 3 + 4 * i)
                act.activation(WH[:, s, :], RAW[:, s, :], ACT.Copy).then_inc(h_ready, 1)

            def wait_tile(stage, group, n, last_unit):
                if n < 2:
                    act.wait_ge(bank_done, BD[stage] + group + 1)
                else:
                    act.wait_ge(w_used, last_unit + 1)

            def norm(n):
                for j in range(KT):
                    act.wait_ge(x_ready, KT * n + j + 1)
                    act.activation(TMP[:, j, :], X[:, j, :], ACT.Square).then_inc(sq_ready, 1)
                act.wait_ge(ssq_ready, n + 1)
                act.activation(STD[:, :], AUX[:, 0, :], ACT.Sqrt, bias=cc(C_EPS)).then_inc(std_ready, 1)
                for j in range(KT):
                    act.wait_ge(t_ready, KT * n + j + 1)
                    shift = mod(n // 2, 3 * (n % 2), j)
                    if n == 6:
                        act.activation(XO[:, j, :], TMP[:, j, :], ACT.Identity, bias=shift).then_inc(xo_ready, 1)
                    else:
                        act.activation(XH[:, j, :], TMP[:, j, :], ACT.Identity, bias=shift).then_inc(hh_ready, 1)

            def feed_forward(layer):
                base, m0, td = U0[f"gu{layer}"], FT * layer, BD[f"gu{layer}"]

                def gates(i, g):
                    for n in range(2):
                        act.wait_ge(bank_done, i * 2 + td + g + 1)
                        act.activation(TMP[:, 2 * g + n, :], M[:, 4 * g + n, :], ACT.Silu).then_inc(silu_ready, 1)
                    for n in range(2):
                        act.wait_ge(midf_ready, i * 4 + m0 + 2 * g + n + 1)
                        act.activation(MHF[:, bass.ds((i * 4 + 2 * g + n) * T, T)], TMP[:, 4 + 2 * g + n, :], ACT.Copy).then_inc(midh_ready, 1)

                for k in range(3):
                    high(base, k)
                norm(2 * layer + 1)
                high(base, 3)
                with act.Fori(1, 5) as i:
                    high(base, 0, i)
                    high(base, 1, i)
                    gates(i - 1, 0)
                    high(base, 2, i)
                    high(base, 3, i)
                    gates(i - 1, 1)
                high(base, 20)
                high(base, 21)
                gates(4, 0)
                base = U0[f"dn{layer}"]
                high(base, 0)
                high(base, 1)
                gates(4, 1)
                high(base, 2)
                gates(5, 0)
                with act.Fori(0, 2) as i:
                    for k in range(3, 7):
                        high(base, k, i)

            act.wait_ge(c_turned, 1)
            act.activation(COND[:, :], AUX[:, 0, 0:2 * KT], ACT.Silu).then_inc(cond_ready, 1)
            for j in range(KT):
                act.wait_ge(x_turned, j // 2 + 1)
                act.activation(X[:, j, :], M[:, j, :], ACT.Copy).then_inc(x_ready, 1)
            act.wait_ge(rows_turned, 1)
            act.activation(VC[:, :], AUX[:, 2:4, :].rearrange("p a t -> p (a t)")[:, 0:N_ROWS], ACT.Copy).then_inc(vc_ready, 1)
            act.wait_ge(ang_v, 10)
            act.activation(SIN[:, :], ANG[:, 0, :], ACT.Sin).then_inc(ang_s, 1)
            act.activation(COS[:, :], ANG[:, 1, :], ACT.Sin, bias=cc(C_HALFPI)).then_inc(ang_s, 1)
            norm(0)
            for k in range(4):
                high(U0["qkv_a"], k)

            def qa_square(i):
                stage_tile = [("qkv_a", 0, i, 1), ("qkv_a", 1, i - 4, 3)][i // 4] if i < 8 else None
                if stage_tile:
                    wait_tile(*stage_tile)
                if i >= 2:
                    act.wait_ge(qa_ssq, i - 1)
                act.activation(QSQ[:, i % 2, :], M[:, i % 8, :], ACT.Square).then_inc(qa_sq, 1)

            def qa_root(i):
                act.wait_ge(qa_ssq, i + 1)
                if i >= 2:
                    act.wait_ge(qa_rs, i - 1)
                act.activation(QSTD[:, i % 2, :], AUX[:, 2 * (i % 2), :], ACT.Sqrt, bias=cc(C_EPS)).then_inc(qa_std, 1)

            high(U0["qkv_a"], 4)
            for i in range(4):
                qa_square(i)
                if i >= 1:
                    qa_root(i - 1)
            qa_root(3)
            high(U0["wo_a"], 0)
            for i in range(4, 9):
                if i == 8:
                    act.wait_ge(w_used, 5)
                    act.activation(VA[:, :, :], M[:, 1, :].rearrange("p (m d) -> p m d", m=2), ACT.Copy).then_inc(va_ready, 1)
                qa_square(i)
                if i >= 5:
                    qa_root(i - 1)
            qa_root(8)
            high(U0["wo_a"], 1)
            high(U0["wo_a"], 2)
            high(U0["wo_a"], 3)
            act.wait_ge(ks_t, 1)
            act.activation(KS[:, :], AUX[:, 4, :], ACT.Copy).then_inc(ks_ready, 1)

            def sa_exp(b):
                act.wait_ge(sa_nm, b + 1)
                if b >= 2:
                    act.wait_ge(sa_tr, 2 * (b - 1))
                for e in range(2):
                    for blk, lo, hi in ((0, 0, P), (1, P, 3 * P)):
                        act.activation(PR[:, b % 2, e, lo:hi], MB[:, 2 * (b % 2) + e, lo:hi], ACT.Exp,
                                       bias=SM[:, b % 2, 1, 2 * e + blk:2 * e + blk + 1],
                                       accum_out=RS_SUM[:, b % 2, 2 * e + blk:2 * e + blk + 1]).then_inc(sa_p, 1)
                act.wait_ge(sa_d, b + 1)
                act.activation(SM[:, b % 2, 3, :], SM[:, b % 2, 2, :], ACT.Exp).then_inc(sa_e, 1)

            sa_exp(0)
            sa_exp(1)
            for b in range(8):
                for e in range(2):
                    act.wait_ge(sa_tr, 2 * b + e + 1)
                    if b >= 2:
                        act.wait_ge(sa_o, b - 1)
                    act.activation(PT[:, b % 2, e, :], AB4[:, e, 0:384], ACT.Copy).then_inc(sa_ptc, 1)
                if b + 2 < 8:
                    sa_exp(b + 2)
                act.wait_ge(sa_o, b + 1)
                act.activation(XH[:, b, :], AUX[:, 4, :], ACT.Copy).then_inc(hh_ready, 1)
            feed_forward(0)

            base = U0["qkv_b"]

            def qb_copy(g):
                if g < 4:
                    dst = QB if g < 2 else KB
                    for n in range(4):
                        wait_tile("qkv_b", g, n, base + 2 * g + 1)
                        act.activation(dst[:, 4 * (g % 2) + n, :], M[:, 4 * (g % 2) + n, :], ACT.Copy,
                                       scale=SCALE if g < 2 else 1.0).then_inc(qb_ev, 1)
                else:
                    for m in range(2):
                        if m == 0:
                            act.wait_ge(bank_done, BD["qkv_b"] + g + 1)
                        else:
                            act.wait_ge(w_used, base + 2 * g + 2)
                        act.activation(VB[:, m, 512 * (g - 4):512 * (g - 4) + 512], MB[:, 2 * (g % 2) + m, :], ACT.Copy).then_inc(qb_ev, 1)

            for k in range(3):
                high(base, k)
            norm(2)
            high(base, 3)
            for g in range(2, 6):
                high(base, 2 * g)
                high(base, 2 * g + 1)
                qb_copy(g - 2)
            for k in range(2):
                high(U0["wo_b"], k)
            qb_copy(4)
            for k in range(2, 4):
                high(U0["wo_b"], k)
            qb_copy(5)

            def sb_softplus(h):
                act.wait_ge(sb_az, h + 1)
                act.activation(EX[:, h % 2, :], AZ[:, h % 2, :], ACT.Exp).then_inc(sb_ex, 1)
                act.wait_ge(sb_ex, h + 1)
                if h >= 2:
                    act.wait_ge(sb_sp, h - 1)
                act.activation(LN[:, h % 2, :], EX[:, h % 2, :], ACT.Ln, bias=cc(C_ONE)).then_inc(sb_ln, 1)

            def sb_weights(h):
                act.wait_ge(sb_e, h + 1)
                if h >= 2:
                    act.wait_ge(sb_o, h - 1)
                act.activation(AB[:, h % 2, :], MB[:, h % 4, 0:384], ACT.Exp).then_inc(sb_a, 1)

            def sb_high(t):
                act.wait_ge(sb_o, 2 * t + 2)
                act.activation(XH[:, t, :], AUX[:, 4 - 4 * (t % 2), :], ACT.Copy).then_inc(hh_ready, 1)

            for h in range(16 + 2):
                if h < 16:
                    sb_softplus(h)
                if 1 <= h <= 16:
                    sb_weights(h - 1)
                if h >= 2 and h % 2 == 1:
                    sb_high((h - 3) // 2)
            feed_forward(1)

            base = U0["w_in"]
            for k in range(3):
                high(base, k)
            norm(4)
            high(base, 3)
            act.wait_ge(mx_wt_t, 1)
            for q in range(2):
                act.activation(WT[:, 4 * q:4 * q + 4, :], AB4[:, q, :].rearrange("p (h t) -> p h t", h=4), ACT.Copy).then_inc(mx_wt, 1)
            high(base, 4)
            high(base, 5)
            for j in range(4):
                wait_tile("w_in", 0, j, base + 1)
                act.activation(SG[:, j, :], M[:, j, :], ACT.Sigmoid, bias=vc("b_in_2", 12 + j)).then_inc(mx_sg, 1)
            high(base, 6)
            high(base, 7)
            for k in range(2):
                high(U0["w_out"], k)
            for m in range(2):
                act.wait_ge(v_x, m + 1)
                act.activation(VN[:, m, :], VX[:, m, :], ACT.Gelu, accum_out=VST[:, m, 0:1]).then_inc(v_g, 1)
            for k in range(2, 4):
                high(U0["w_out"], k)
            for j in range(4):
                wait_tile("w_in", 3, j, base + 7)
                act.activation(UG[:, j, :], M[:, 4 + j, :], ACT.Gelu, bias=vc("b_in_2", j)).then_inc(ug_ready, 1)
            for m in range(2):
                act.wait_ge(v_c, m + 1)
                act.activation(VN[:, m, :], VX[:, m, :], ACT.Square, accum_out=VST[:, m, 2:3]).then_inc(v_s2, 1)
            for m in range(2):
                act.wait_ge(v_s2, m + 1)
                act.activation(VST[:, m, 3:4], VST[:, m, 2:3], ACT.Sqrt, scale=1.0 / DA, bias=cc(C_EPS)).then_inc(v_sd, 1)
            for j in range(4):
                act.wait_ge(ya_ready, j + 1)
                act.activation(TMP[:, j, :], UG[:, j, :], ACT.Square).then_inc(on_sq, 1)
            act.wait_ge(on_ssq, 1)
            act.activation(STD[:, :], AUX[:, 4, :], ACT.Sqrt, scale=float(D // DA), bias=cc(C_EPS)).then_inc(on_std, 1)
            for j in range(4):
                act.wait_ge(on_t, j + 1)
                act.activation(XH[:, j, :], TMP[:, j, :], ACT.Copy).then_inc(hh_ready, 1)
            for j in range(4):
                act.wait_ge(gn_c, j + 1)
                act.activation(TMP[:, 4 + j, :], CV[:, j, :], ACT.Square).then_inc(gn_sq, 1)
            for j in range(4):
                act.wait_ge(gn_var, j // 2 + 1)
                act.activation(Y0[:, j, 0:T], AUX[:, j, :], ACT.Sqrt, bias=cc(C_EPS)).then_inc(gn_std, 1)
            for j in range(4):
                act.wait_ge(gn_n, j + 1)
                act.activation(SG[:, j, :], CV[:, j, :], ACT.Silu, scale=vc("b_gn_g_2", j), bias=vc("b_gn_b_2", j)).then_inc(yb_ready, 1)
            for j in range(4):
                act.wait_ge(yb_ready, j + 1)
                act.activation(TMP[:, 4 + j, :], SG[:, j, :], ACT.Square).then_inc(on_sq, 1)
            act.wait_ge(on_ssq, 2)
            act.wait_ge(on_rs, 1)
            act.activation(STD[:, :], AUX[:, 5, :], ACT.Sqrt, scale=float(D // DA), bias=cc(C_EPS)).then_inc(on_std, 1)
            for j in range(4):
                act.wait_ge(on_t, 4 + j + 1)
                act.activation(XH[:, 4 + j, :], TMP[:, 4 + j, :], ACT.Copy).then_inc(hh_ready, 1)
            feed_forward(2)

            norm(6)
            for q in range(4):
                act.wait_ge(o_turned, q + 1)
                act.activation(OUT[:, q // 2, 512 * (q % 2):512 * (q % 2) + 512], MB[:, q, :], ACT.Copy).then_inc(o_copied, 1)

        @block.vector
        def _(dve):
            MODS_BY_NORM = [4, 10, 18, 22, 30, 34, 40]
            GAINS = [("norm1_g", 0), ("norm2_g", 0), ("norm1_g", 8), ("norm2_g", 8), ("norm1_g_2", 0),
                     ("norm2_g_2", 0), ("norm_f_g", 0)]

            def low(base, k, i=0):
                s = slot(base, k)
                dve.wait_ge(h_ready, base + k + 1 + 4 * i)
                dve.tensor_tensor(WL[:, s, :], RAW[:, s, :], WH[:, s, :], ALU.subtract).then_inc(l_ready, 1)

            def ada_sum(b, second, i=0):
                for kt in range(KT):
                    w = ADA[:, kt // 4, kt % 4, :]
                    scale = COND[:, KT * second + kt:KT * second + kt + 1]
                    if kt % 4 == 0:
                        dve.wait_ge(a_landed[kt // 4], 16 * (b + 1) + 16 * i)
                    if kt == 0 and b > 0:
                        dve.wait_ge(acc_red, b + i)
                    if kt < 2:
                        dve.tensor_scalar(ACC[:, kt, :], w, scale, None, ALU.mult).then_inc(a_chain, 1)
                    else:
                        dve.wait_ge(a_chain, 8 * b + kt - 1 + 8 * i)
                        dve.scalar_tensor_tensor(out=ACC[:, kt % 2, :], in0=w, scalar=scale, in1=ACC[:, kt % 2, :],
                                                 op0=ALU.mult, op1=ALU.add).then_inc(a_chain, 1)

            def ada_bias(b, ident, i=0):
                dve.wait_ge(acc_red, b + 1 + i)
                at = bass.ds(i * 4 + 4 * ident, 4)
                dve.tensor_tensor(MOD[:, at], ADP, VC[:, at], ALU.add).then_inc(mod_ready, 1)

            def wait_tile(stage, group, n, last_unit):
                if n < 2:
                    dve.wait_ge(bank_done, BD[stage] + group + 1)
                else:
                    dve.wait_ge(w_used, last_unit + 1)

            def add_tile(version, layer, chunk, j, mods):
                if j == 0:
                    dve.wait_ge(mod_ready, mods)
                dve.scalar_tensor_tensor(out=X[:, j, :], in0=M[:, j, :], scalar=mod(layer, chunk, j), in1=X[:, j, :],
                                         op0=ALU.mult, op1=ALU.add).then_inc(x_ready, 1)

            def norm(n):
                dve.wait_ge(mod_ready, MODS_BY_NORM[n])
                if n > 0:
                    dve.wait_ge(t_ready, KT * n)
                else:
                    dve.wait_ge(vc_ready, 1)
                name, at = GAINS[n]
                dve.scalar_tensor_tensor(out=COEF[:, :], in0=mod(n // 2, 3 * (n % 2) + 1, 0, KT), scalar=1.0,
                                         in1=vc(name, at, KT), op0=ALU.add, op1=ALU.mult).then_inc(coef_ready, 1)
                dve.wait_ge(std_ready, n + 1)
                dve.reciprocal(RSTD[:, :], STD[:, :]).then_inc(rstd_ready, 1)
                dve.wait_ge(coef_ready, n + 1)
                dve.wait_ge(rstd_ready, n + 1)
                fill = 3 * (n // 2) + 2 * (n % 2)
                for j in range(KT + 2):
                    if j < KT:
                        dve.scalar_tensor_tensor(out=TMP[:, j, :], in0=X[:, j, :], scalar=COEF[:, j:j + 1], in1=RSTD[:, :],
                                                 op0=ALU.mult, op1=ALU.mult).then_inc(t_ready, 1)
                    if j >= 2 and n < 6:
                        q = j - 2
                        dve.wait_ge(hh_ready, KT * fill + q + 1)
                        dve.scalar_tensor_tensor(out=XL[:, q, :], in0=TMP[:, q, :], scalar=mod(n // 2, 3 * (n % 2), q),
                                                 in1=XH[:, q, :], op0=ALU.add, op1=ALU.subtract).then_inc(xin_ready, 1)

            def feed_forward(layer, before):
                base, m0 = U0[f"gu{layer}"], FT * layer
                b0, id0, steps = GU_BLOCKS[layer]
                second = int(layer >= 1)

                def products(i, g):
                    for n in range(2):
                        m = i * 4 + (m0 + 2 * g + n)
                        dve.wait_ge(silu_ready, m + 1)
                        dve.wait_ge(w_used, i * 4 + U0[f"gu{layer}"] + 2 * g + 2)
                        dve.tensor_tensor(TMP[:, 4 + 2 * g + n, :], TMP[:, 2 * g + n, :], M[:, 4 * g + 2 + n, :],
                                          ALU.mult).then_inc(midf_ready, 1)
                    for n in range(2):
                        m = i * 4 + (2 * g + n)
                        dve.wait_ge(midh_ready, m + m0 + 1)
                        at = bass.ds(m * T, T)
                        dve.tensor_tensor(MLF[:, at], TMP[:, 4 + 2 * g + n, :], MHF[:, at], ALU.subtract).then_inc(mid_ready, 1)

                for k in range(3):
                    low(base, k)
                before()
                norm(2 * layer + 1)
                low(base, 3)
                if 0 in steps:
                    ada_sum(b0, second)
                    ada_bias(b0, id0)
                with dve.Fori(1, 5) as i:
                    at = i - steps[0]
                    ada_sum(b0, second, at)
                    low(base, 0, i)
                    low(base, 1, i)
                    products(i - 1, 0)
                    low(base, 2, i)
                    low(base, 3, i)
                    ada_bias(b0, id0, at)
                    products(i - 1, 1)
                if 5 in steps:
                    ada_sum(b0 + 5, second)
                low(base, 20)
                low(base, 21)
                if 5 in steps:
                    ada_bias(b0 + 5, id0 + 5)
                products(4, 0)
                base = U0[f"dn{layer}"]
                low(base, 0)
                low(base, 1)
                products(4, 1)
                low(base, 2)
                products(5, 0)
                b0, id0 = DN_BLOCKS[layer]
                with dve.Fori(0, 2) as i:
                    ada_sum(b0, int(layer == 2), i)
                    low(base, 3, i)
                    low(base, 4, i)
                    low(base, 5, i)
                    low(base, 6, i)
                    ada_bias(b0, id0, i)

            def add_down(layer, mods):
                def go():
                    for j in range(KT):
                        if j < KT - 2:
                            dve.wait_ge(bank_done, BD[f"dn{layer}"] + 3 + j // 2 + 1)
                        else:
                            dve.wait_ge(w_used, U0[f"dn{layer}"] + 11)
                        add_tile(2 * layer + 2, layer, 5, j, mods)
                return go

            def add_out(stage, layer, g, mods):
                for n in range(4):
                    wait_tile(stage, g, n, U0[stage] + 2 * g + 1)
                    add_tile(2 * layer + 1, layer, 2, 4 * g + n, mods)

            dve.wait_ge(const_in, 16)
            dve.tensor_copy(IDB[:, :], IDENT).then_inc(masks_ready, 1)
            dve.wait_ge(misc_in, 64)
            dve.tensor_copy(MASKA[:, :], CTMP[:, T0["mask_a"]:T0["mask_a"] + 3 * P]).then_inc(masks_ready, 1)
            dve.tensor_copy(MASKB[:, :], CTMP[:, T0["mask_b"]:T0["mask_b"] + P]).then_inc(masks_ready, 1)
            dve.tensor_scalar(NSINK[:, :, :], SINK[:, :, :], -1.0, None, ALU.mult).then_inc(sink_ready, 1)
            A0, A1, A2, A3 = (ANG[:, q, :] for q in range(4))
            dve.tensor_copy(A3, POSI[:, :]).then_inc(ang_v, 1)
            dve.wait_ge(ang_v, 1)
            dve.tensor_scalar(A0, A3, cc(C_INVF), None, ALU.mult).then_inc(ang_v, 1)
            dve.wait_ge(ang_v, 2)
            dve.tensor_scalar(A1, A0, float(1 / (2 * np.pi)), ROUND, ALU.mult, ALU.add).then_inc(ang_v, 1)
            dve.wait_ge(ang_v, 3)
            dve.tensor_scalar(A2, A1, -ROUND, None, ALU.add).then_inc(ang_v, 1)
            for q, part in enumerate(two_pi_parts()):
                dve.wait_ge(ang_v, 4 + q)
                src, dst = (A0, A1) if q % 2 == 0 else (A1, A0)
                dve.scalar_tensor_tensor(out=dst, in0=A2, scalar=-part, in1=src, op0=ALU.mult, op1=ALU.add).then_inc(ang_v, 1)
            dve.wait_ge(ang_v, 8)
            dve.tensor_scalar(A0, A0, 3.1415925, -3.1415925, ALU.min, ALU.max).then_inc(ang_v, 1)
            dve.wait_ge(ang_v, 9)
            dve.scalar_tensor_tensor(out=A1, in0=A0, scalar=-1.0, in1=A0, op0=ALU.mult, op1=ALU.min).then_inc(ang_v, 1)

            dve.wait_ge(cond_ready, 1)
            for b, ident in enumerate(FIRST_IDS):
                ada_sum(b, 0)
                if b == 0:
                    dve.wait_ge(vc_ready, 1)
                ada_bias(b, ident)
            dve.wait_ge(ang_s, 2)
            dve.tensor_scalar(COS[:, :], COS[:, :], cc(C_ROPE), cc(C_KEEP), ALU.mult, ALU.add).then_inc(trig_ready, 1)
            dve.tensor_scalar(vc("q_norm_a", 0), vc("q_norm_a", 0), SCALE, None, ALU.mult).then_inc(gain_ready, 1)
            norm(0)
            base = U0["qkv_a"]
            for k in range(4):
                low(base, k)

            def qa_recip(i):
                dve.wait_ge(qa_std, i + 1)
                if i >= 2:
                    dve.wait_ge(qa_n, i - 1)
                dve.reciprocal(QRS[:, i % 2, :], QSTD[:, i % 2, :]).then_inc(qa_rs, 1)

            def qa_norm(i):
                dve.wait_ge(qa_rs, i + 1)
                if i >= 2:
                    dve.wait_ge(qa_rot, i - 1)
                    dve.wait_ge(qa_c, i - 1)
                dve.wait_ge(qa_sq, min(i + 2 - i % 2, 9))
                gain = vc("q_norm_a", 0) if i < 8 else vc("k_norm_a", 0)
                dve.scalar_tensor_tensor(out=QN[:, i % 2, :], in0=M[:, i % 8, :], scalar=gain, in1=QRS[:, i % 2, :],
                                         op0=ALU.mult, op1=ALU.mult).then_inc(qa_n, 1)

            def qa_rope(i):
                dve.wait_ge(qa_n, i + 1)
                dve.tensor_tensor(QA[:, i, :], QN[:, i % 2, :], COS[:, :], ALU.mult).then_inc(qa_c, 1)
                dve.wait_ge(qa_rot, i + 1)
                if i >= 2:
                    dve.wait_ge(qa_q, i - 1)
                dve.tensor_tensor(QT2[:, i % 2, :], AUX[:, 4, :], SIN[:, :], ALU.mult).then_inc(qa_t2, 1)

            def qa_add(i):
                dve.wait_ge(qa_t2, i + 1)
                dve.tensor_tensor(QA[:, i, :], QA[:, i, :], QT2[:, i % 2, :], ALU.add).then_inc(qa_q, 1)

            dve.wait_ge(gain_ready, 1)
            dve.wait_ge(trig_ready, 1)
            ada_sum(4, 0)
            low(base, 4)
            for tiles in (range(0, 4), range(4, 9)):
                for i in tiles:
                    qa_recip(i)
                    qa_norm(i)
                    if i > tiles[0]:
                        qa_rope(i - 1)
                        qa_add(i - 1)
                qa_rope(tiles[-1])
                qa_add(tiles[-1])
                if tiles[0] == 0:
                    ada_bias(4, 4)
                    ada_sum(5, 0)
                    low(U0["wo_a"], 0)
            ada_bias(5, 5)
            low(U0["wo_a"], 1)
            low(U0["wo_a"], 2)
            low(U0["wo_a"], 3)

            def sa_max(b):
                p = b % 2
                if b >= 2:
                    dve.wait_ge(sa_r, b - 1)
                dve.wait_ge(sa_s, b + 1)
                for blk, lo, hi in ((0, 0, P), (1, P, 3 * P)):
                    dve.reduce_max(SM[:, p, 0, blk:4:2], MB[:, 2 * p:2 * p + 2, lo:hi], AX_X).then_inc(sa_m, 1)
                dve.wait_ge(sa_m, 2 * b + 2)
                if b == 0:
                    dve.wait_ge(sink_ready, 1)
                if b >= 2:
                    dve.wait_ge(sa_e, b - 1)
                nsink = NSINK[:, :, 2 * b:2 * b + 2].rearrange("p k e -> p e k")
                sink = SINK[:, :, 2 * b:2 * b + 2].rearrange("p k e -> p e k")

                def small(row):
                    return SM[:, p, row, :].rearrange("p (e k) -> p e k", k=2)

                dve.scalar_tensor_tensor(out=small(1), in0=small(0), scalar=-1.0, in1=nsink,
                                         op0=ALU.mult, op1=ALU.min).then_inc(sa_nm, 1)
                dve.wait_ge(sa_nm, b + 1)
                dve.tensor_tensor(small(2), sink, small(1), ALU.add).then_inc(sa_d, 1)

            def sa_divide(b):
                p = b % 2
                dve.wait_ge(sa_p, 4 * b + 4)
                dve.wait_ge(sa_e, b + 1)
                if b >= 2:
                    dve.wait_ge(sa_pn, 4 * b - 4)
                dve.tensor_tensor(SM[:, p, 4, :], RS_SUM[:, p, :], SM[:, p, 3, :], ALU.add).then_inc(sa_t, 1)
                dve.wait_ge(sa_t, b + 1)
                dve.reciprocal(SM[:, p, 5, :], SM[:, p, 4, :]).then_inc(sa_r, 1)
                dve.wait_ge(sa_r, b + 1)
                for e in range(2):
                    for blk, lo, hi in ((0, 0, P), (1, P, 3 * P)):
                        dve.tensor_scalar(PR[:, p, e, lo:hi], PR[:, p, e, lo:hi], SM[:, p, 5, 2 * e + blk:2 * e + blk + 1],
                                          None, ALU.mult).then_inc(sa_pn, 1)

            def attn_low(fill, b):
                dve.wait_ge(hh_ready, KT * fill + b + 1)
                o = AUX[:, 4, :] if fill == 1 else AUX[:, 4 - 4 * (b % 2), :]
                dve.tensor_tensor(XL[:, b, :], o, XH[:, b, :], ALU.subtract).then_inc(xin_ready, 1)

            sa_max(0)
            sa_max(1)
            for b in range(8):
                sa_divide(b)
                if b + 2 < 8:
                    sa_max(b + 2)
                if b % 2 == 1:
                    if b > 1:
                        ada_bias(4 + b // 2 + 1, 4 + b // 2 + 1)
                    ada_sum(4 + b // 2 + 2, 0)
                attn_low(1, b)
            ada_bias(9, 9)
            add_out("wo_a", 0, 0, 6)
            feed_forward(0, lambda: add_out("wo_a", 0, 1, 6))

            base = U0["qkv_b"]
            for k in range(3):
                low(base, k)
            add_down(0, 18)()
            norm(2)
            low(base, 3)
            ada_sum(18, 0)
            for k in range(4, 8):
                low(base, k)
            ada_bias(18, 18)
            for q in range(2):
                ada_sum(19 + q, 0)
                low(base, 8 + 2 * q)
                low(base, 9 + 2 * q)
                ada_bias(19 + q, 19 + q)
            ada_sum(21, 0)
            for k in range(2):
                low(U0["wo_b"], k)
            ada_bias(21, 21)
            for k in range(2, 4):
                low(U0["wo_b"], k)

            def sb_abs(h):
                z = MB[:, h % 4, 0:384]
                dve.wait_ge(sb_z, h + 1)
                if h >= 2:
                    dve.wait_ge(sb_sp, h - 1)
                dve.tensor_scalar(ZP[:, h % 2, :], z, 0.0, None, ALU.max).then_inc(sb_zp, 1)
                dve.wait_ge(sb_zp, h + 1)
                if h >= 2:
                    dve.wait_ge(sb_ex, h - 1)
                dve.scalar_tensor_tensor(out=AZ[:, h % 2, :], in0=ZP[:, h % 2, :], scalar=-2.0, in1=z,
                                         op0=ALU.mult, op1=ALU.add).then_inc(sb_az, 1)

            def sb_plus(h):
                dve.wait_ge(sb_ln, h + 1)
                if h >= 2:
                    dve.wait_ge(sb_e, h - 1)
                dve.tensor_tensor(SP[:, h % 2, :], ZP[:, h % 2, :], LN[:, h % 2, :], ALU.add).then_inc(sb_sp, 1)

            for h in range(16 + 3):
                if h < 16:
                    sb_abs(h)
                if 1 <= h <= 16:
                    sb_plus(h - 1)
                if h >= 3 and h % 2 == 1:
                    attn_low(4, (h - 3) // 2)
            add_out("wo_b", 1, 0, 16)
            feed_forward(1, lambda: add_out("wo_b", 1, 1, 16))

            base = U0["w_in"]
            for k in range(3):
                low(base, k)
            add_down(1, 30)()
            norm(4)
            low(base, 3)
            ada_sum(30, 1)
            dve.wait_ge(mx_in, 112)
            dve.tensor_tensor(WSP[:, :, :], WSP[:, :, :], TRIL[:, :].unsqueeze(1).to_broadcast([P, 8, P]), ALU.mult).then_inc(mx_tril, 1)
            dve.memset(Y0[:, :, 0:CONV - 1], 0.0).then_inc(mx_pad, 1)
            low(base, 4)
            low(base, 5)
            for j in range(4):
                dve.wait_ge(mx_sg, j + 1)
                wait_tile("w_in", 1, j, base + 3)
                dve.scalar_tensor_tensor(out=Y0[:, j, CONV - 1:], in0=M[:, 4 + j, :], scalar=vc("b_in_2", 8 + j), in1=SG[:, j, :],
                                         op0=ALU.add, op1=ALU.mult).then_inc(mx_y0, 1)
            ada_bias(30, 30)
            low(base, 6)
            low(base, 7)
            ada_sum(31, 1)
            for k in range(2):
                low(U0["w_out"], k)

            def tap(k, j):
                at = bass.ds(k, T) if not isinstance(k, int) else slice(k, k + T)
                w = COL["b_conv_w_2"] + j
                return Y0[:, j, at], VC[:, bass.ds(k * 4 + w, 1)]

            def taps(lo, hi):
                with dve.Fori(lo, hi) as k:
                    for j in range(4):
                        src, w = tap(k, j)
                        dve.wait_ge(cv_c, k * 4 + (j - 3))
                        dve.scalar_tensor_tensor(out=CV[:, j, :], in0=src, scalar=w, in1=CV[:, j, :],
                                                 op0=ALU.mult, op1=ALU.add).then_inc(cv_c, 1)

            dve.wait_ge(mx_pad, 1)
            dve.wait_ge(mx_y0, 4)
            for j in range(4):
                src, w = tap(0, j)
                dve.tensor_scalar(CV[:, j, :], src, w, vc("b_conv_b_2", j), ALU.mult, ALU.add).then_inc(cv_c, 1)
            taps(1, 8)
            for m in range(2):
                if m == 0:
                    dve.wait_ge(bank_done, BD["w_in"] + 3)
                else:
                    dve.wait_ge(w_used, base + 6)
                dve.tensor_tensor(VX[:, m, :], MB[:, m, :], BV[:, :], ALU.add).then_inc(v_x, 1)
            taps(8, 20)
            for m in range(2):
                dve.wait_ge(v_g, m + 1)
                dve.tensor_scalar(VST[:, m, 1:2], VST[:, m, 0:1], 1.0 / DA, None, ALU.mult).then_inc(v_mu, 1)
            for m in range(2):
                dve.wait_ge(v_mu, m + 1)
                dve.tensor_scalar(VX[:, m, :], VN[:, m, :], VST[:, m, 1:2], None, ALU.subtract).then_inc(v_c, 1)
            ada_bias(31, 31)
            ada_sum(32, 1)
            for k in range(2, 4):
                low(U0["w_out"], k)
            taps(20, CONV)
            for m in range(2):
                dve.wait_ge(v_sd, m + 1)
                dve.reciprocal(VST[:, m, 4:5], VST[:, m, 3:4]).then_inc(v_rs, 1)
            for m in range(2):
                dve.wait_ge(v_rs, m + 1)
                dve.scalar_tensor_tensor(out=VN[:, m, :], in0=VX[:, m, :], scalar=VST[:, m, 4:5], in1=LNG[:, :],
                                         op0=ALU.mult, op1=ALU.mult).then_inc(v_n, 1)
            for m in range(2):
                dve.wait_ge(v_n, m + 1)
                dve.tensor_tensor(VN[:, m, :], VN[:, m, :], LNB[:, :], ALU.add).then_inc(v_b, 1)
            ada_bias(32, 32)
            ada_sum(33, 1)
            for j in range(4):
                dve.wait_ge(sp_done, j // 2 + 1)
                bias = BSB[:, j, :].unsqueeze(1).to_broadcast([P, 2, P])
                dve.tensor_tensor(TMP[:, j, :].rearrange("p (c t) -> p c t", c=2), M[:, j, :].rearrange("p (c t) -> p c t", c=2),
                                  bias, ALU.add).then_inc(ya_t, 1)
            for j in range(4):
                dve.wait_ge(ya_t, j + 1)
                dve.wait_ge(ug_ready, j + 1)
                dve.tensor_tensor(UG[:, j, :], TMP[:, j, :], UG[:, j, :], ALU.mult).then_inc(ya_ready, 1)
            for j in range(4):
                dve.wait_ge(gn_mu, j // 2 + 1)
                dve.tensor_tensor(CV[:, j, :], CV[:, j, :], AUX[:, j, :], ALU.subtract).then_inc(gn_c, 1)

            def out_norm(q, rows, name):
                dve.wait_ge(on_std, q + 1)
                if q == 1:
                    dve.wait_ge(on_t, 4)
                dve.reciprocal(RSTD[:, :], STD[:, :]).then_inc(on_rs, 1)
                dve.wait_ge(on_rs, q + 1)
                for j in range(4):
                    dve.scalar_tensor_tensor(out=TMP[:, 4 * q + j, :], in0=rows[:, j, :], scalar=vc(name, j), in1=RSTD[:, :],
                                             op0=ALU.mult, op1=ALU.mult).then_inc(on_t, 1)
                for j in range(4):
                    dve.wait_ge(hh_ready, KT * 7 + 4 * q + j + 1)
                    dve.tensor_tensor(XL[:, 4 * q + j, :], TMP[:, 4 * q + j, :], XH[:, 4 * q + j, :], ALU.subtract).then_inc(xin_ready, 1)

            out_norm(0, UG, "out_norm_a_g_2")
            for j in range(4):
                dve.wait_ge(gn_std, j + 1)
                dve.reciprocal(Y0[:, j, 0:T], Y0[:, j, 0:T]).then_inc(gn_rs, 1)
                dve.wait_ge(gn_rs, j + 1)
                dve.tensor_tensor(CV[:, j, :], CV[:, j, :], Y0[:, j, 0:T], ALU.mult).then_inc(gn_n, 1)
            ada_bias(33, 33)
            out_norm(1, SG, "out_norm_b_g_2")
            add_out("w_out", 2, 0, 28)
            feed_forward(2, lambda: add_out("w_out", 2, 1, 28))
            add_down(2, 40)()
            norm(6)

        @block.tensor
        def _(pe):
            def three(out_ap, wh, wl, xh, xl, start, stop):
                pe.matmul(out_ap, wh, xh, start=start, stop=False, skip_group_check=True)
                pe.matmul(out_ap, wh, xl, start=False, stop=False, skip_group_check=True)
                return pe.matmul(out_ap, wl, xh, start=False, stop=stop, skip_group_check=True)

            def unit(base, k, i, taus, kts, x_of, first, last, by_rows=None):
                s = slot(base, k)
                pe.wait_ge(l_ready, base + k + 1 + 4 * i)
                width = 2048 // len(kts)
                pairs = [(q, n) for n in range(len(taus)) for q in range(len(kts))]
                if by_rows is not None:
                    pairs = [(q, n) for q in range(len(kts)) for n in range(len(taus))]
                for at, (q, n) in enumerate(pairs):
                    if by_rows is not None and n == 0:
                        pe.wait_ge(xin_ready, KT * by_rows + kts[q] + 1)
                    tau, col = taus[n]
                    xh, xl = x_of(kts[q])
                    cols = slice(q * width + col, q * width + col + P)
                    ends = last and q == len(kts) - 1
                    mm = three(M[:, tau, :], WH[:, s, cols], WL[:, s, cols], xh, xl,
                               first and q == 0 and tau % 2 == 0, ends)
                    if at == len(pairs) - 1:
                        mm.then_inc(w_used, 1)
                    elif ends and tau % 2 == 1:
                        mm.then_inc(bank_done, 1)

            def operand(kt):
                return XH[:, kt, :], XL[:, kt, :]

            def group(base, g, st, i=0, fill=None):
                taus = [(4 * st + n, n * P) for n in range(4)]
                unit(base, 2 * g, i, taus, range(0, 4), operand, True, False, fill)
                if fill is not None:
                    pe.wait_ge(xin_ready, KT * fill + KT)
                unit(base, 2 * g + 1, i, taus, range(4, 8), operand, False, True)

            def values(base, k, kts, col, width, outs, first, last):
                s = slot(base, k)
                pe.wait_ge(l_ready, base + k + 1)
                row = 2048 // len(kts)
                for m in range(2):
                    for q, kt in enumerate(kts):
                        rows = slice(m * P, m * P + P)
                        wh, wl = (w[:, s, q * row + col:q * row + col + width] for w in (WH, WL))
                        start = first and q == 0 and outs[m][1]
                        ends = last and q == len(kts) - 1
                        pe.matmul(outs[m][0], XH[:, kt, rows], wh, start=start, stop=False, skip_group_check=True)
                        pe.matmul(outs[m][0], XL[:, kt, rows], wh, start=False, stop=False, skip_group_check=True)
                        mm = pe.matmul(outs[m][0], XH[:, kt, rows], wl, start=False, stop=ends, skip_group_check=True)
                    if m == 1:
                        mm.then_inc(w_used, 1)
                    elif last and width == 512:
                        mm.then_inc(bank_done, 1)

            def ada_reduce(b, i=0):
                pe.wait_ge(a_chain, 8 * b + 8 + 8 * i)
                if b > 0:
                    pe.wait_ge(mod_ready, b + i)
                for j in range(4):
                    for q in range(2):
                        mm = pe.matmul(AUX[:, 6, j:j + 1], ACC[:, q, j * P:(j + 1) * P], cc(C_ONE), start=(q == 0), stop=(q == 1))
                mm.then_inc(acc_red, 1)

            def norm(n):
                for j in range(KT):
                    pe.wait_ge(sq_ready, KT * n + j + 1)
                    mm = pe.matmul(AUX[:, 0, :], ONES, TMP[:, j, :], start=(j == 0), stop=(j == KT - 1))
                mm.then_inc(ssq_ready, 1)

            def feed_forward(layer):
                base, m0 = U0[f"gu{layer}"], FT * layer
                b0, id0, steps = GU_BLOCKS[layer]
                norm(2 * layer + 1)
                group(base, 0, 0, 0, 3 * layer + 2)
                if 0 in steps:
                    ada_reduce(b0)
                group(base, 1, 1)
                with pe.Fori(1, 5) as i:
                    ada_reduce(b0, i - steps[0])
                    for g in range(2):
                        pe.wait_ge(midf_ready, i * 4 + m0 + 2 * g - 2)
                        group(base, g, g, i)
                if 5 in steps:
                    ada_reduce(b0 + 5)
                pe.wait_ge(midf_ready, m0 + 18)
                group(base, 10, 0)
                base = U0[f"dn{layer}"]

                def hidden(kt):
                    return MH[:, kt, :], ML[:, kt, :]

                def hidden_at(i, k):
                    def rows(kt):
                        at = bass.ds((i * 8 + kt) * T, T)
                        return MHF[:, at], MLF[:, at]
                    return rows

                pe.wait_ge(midf_ready, m0 + 20)
                pe.wait_ge(mid_ready, m0 + 18)
                down_unit(base, 0, hidden, [4, 5, 6, 7, 0, 1, 2, 3], m0 + 22, True, False)
                for k in (1, 2):
                    down_unit(base, k, hidden, range(8), None, False, False)
                pe.wait_ge(mid_ready, m0 + 22)
                b0, _ = DN_BLOCKS[layer]
                with pe.Fori(0, 2) as i:
                    ada_reduce(b0, i)
                    for k in range(3, 7):
                        down_unit(base, k, hidden_at(i, k), range(8), None, False, k == 6, i)

            def down_unit(base, k, x_of, order, set0_free, first, ending, i=0):
                s = slot(base, k)
                pe.wait_ge(l_ready, base + k + 1 + 4 * i)
                for at, n in enumerate(order):
                    if set0_free is not None and n == 0:
                        pe.wait_ge(midf_ready, set0_free)
                    for q in range(2):
                        xh, xl = x_of(2 * k + q)
                        cols = slice(q * D + n * P, q * D + n * P + P)
                        mm = three(M[:, n, :], WH[:, s, cols], WL[:, s, cols], xh, xl, first and q == 0 and n % 2 == 0, False)
                    if at == KT - 1:
                        mm.then_inc(w_used, 1)
                    elif ending and n % 2 == 1:
                        mm.then_inc(bank_done, 1)

            pe.wait_ge(const_in, 16)
            pe.wait_ge(crows_in, 32)
            pe.transpose(AUX[:, 0, 0:2 * KT], CROWS[:, :], IDENT[0:2 * KT, 0:2 * KT]).then_inc(c_turned, 1)
            pe.wait_ge(x_in, 16)
            for j in range(KT):
                for m in range(2):
                    mm = pe.transpose(M[:, j, m * P:(m + 1) * P], XTOK[:, m, j * P:(j + 1) * P], IDENT)
                if j % 2 == 1:
                    mm.then_inc(x_turned, 1)
            pe.wait_ge(rows_in, 16 * ROW_DMAS)
            for r in range(ROW_TILES):
                n = min(P, N_ROWS - r * P)
                mm = pe.transpose(AUX[:, 2 + r // 2, (r % 2) * P:(r % 2) * P + n], VROWS[0:n, r, :], IDENT[0:n, 0:n])
            mm.then_inc(rows_turned, 1)
            pe.wait_ge(cond_ready, 1)
            norm(0)
            for b in range(4):
                ada_reduce(b)

            base = U0["qkv_a"]

            def qa_mean(i):
                pe.wait_ge(qa_sq, i + 1)
                if i >= 2:
                    pe.wait_ge(qa_std, i - 1)
                pe.matmul(AUX[:, 2 * (i % 2), :], BLK, QSQ[:, i % 2, :], start=True, stop=True).then_inc(qa_ssq, 1)

            def qa_turn(i):
                pe.wait_ge(qa_n, i + 1)
                if i >= 1:
                    pe.wait_ge(qa_t2, i)
                pe.matmul(AUX[:, 4, :], ROTM, QN[:, i % 2, :], start=True, stop=True).then_inc(qa_rot, 1)

            group(base, 0, 0, 0, 0)
            taus = [(4 + n, n * P) for n in range(4)]
            unit(base, 2, 0, taus, range(0, 4), operand, True, False)
            for i in range(4):
                qa_mean(i)
            unit(base, 3, 0, taus, range(4, 8), operand, False, True)
            ada_reduce(4)
            for i in range(4):
                qa_turn(i)
            pe.wait_ge(l_ready, base + 5)
            for kt in range(KT):
                cols = slice(kt * 256, kt * 256 + P)
                three(M[:, 0, :], WH[:, 0, cols], WL[:, 0, cols], *operand(kt), kt == 0, kt == KT - 1)
            values(base, 4, range(8), P, P, [(M[:, 1, 0:P], False), (M[:, 1, P:2 * P], False)], True, True)
            for i in range(4, 9):
                qa_mean(i)
                if i >= 5:
                    qa_turn(i - 1)
            qa_turn(8)
            ada_reduce(5)
            pe.wait_ge(qa_q, 9)
            pe.wait_ge(misc_in, 64)
            pe.matmul(AUX[:, 4, :], CTMP[:, T0["swap"]:T0["swap"] + P], QA[:, 8, :], start=True, stop=True).then_inc(ks_t, 1)

            def sa_scores(b):
                for e in range(2):
                    rows = slice(HD * e, HD * e + HD)
                    keys = QA[rows, 8, :] if e == b // 4 else KS[rows, :]
                    bank = MB[:, 2 * (b % 2) + e, :]
                    pe.matmul(bank[:, 0:P], QA[rows, b, 0:P], keys[:, 0:P], start=True, stop=False, skip_group_check=True)
                    pe.matmul(bank[:, P:3 * P], QA[rows, b, P:2 * P], keys, start=False, stop=False, skip_group_check=True)
                    mm = pe.matmul(bank[:, 0:3 * P], IDB[:, :], MASKA[:, :], start=False, stop=True, skip_group_check=True)
                mm.then_inc(sa_s, 1)

            def sa_turn(b):
                for e in range(2):
                    pe.wait_ge(sa_pn, 4 * b + 2 * e + 2)
                    if b >= 1:
                        pe.wait_ge(sa_ptc, 2 * (b - 1) + e + 1)
                    for blk in range(3):
                        cols = slice(blk * P, blk * P + P)
                        mm = pe.transpose(AB4[:, e, cols], PR[:, b % 2, e, cols], IDENT)
                    mm.then_inc(sa_tr, 1)

            def sa_rows(b):
                kv = slice(HD * (b // 4), HD * (b // 4) + HD)
                if b >= 1:
                    pe.wait_ge(xin_ready, KT + b)
                for e in range(2):
                    pe.wait_ge(sa_ptc, 2 * b + e + 1)
                    rows = slice(HD * e, HD * e + HD)
                    o = AUX[rows, 4, :]
                    pe.matmul(o[:, 0:P], VA[:, 0, kv], PT[:, b % 2, e, 0:P], start=True, stop=True, skip_group_check=True)
                    pe.matmul(o[:, P:2 * P], VA[:, 0, kv], PT[:, b % 2, e, P:2 * P], start=True, stop=False, skip_group_check=True)
                    mm = pe.matmul(o[:, P:2 * P], VA[:, 1, kv], PT[:, b % 2, e, 2 * P:3 * P], start=False, stop=True, skip_group_check=True)
                mm.then_inc(sa_o, 1)

            pe.wait_ge(ks_ready, 1)
            pe.wait_ge(va_ready, 1)
            pe.wait_ge(masks_ready, 3)
            sa_scores(0)
            sa_scores(1)
            for b in range(8):
                sa_turn(b)
                if b + 2 < 8:
                    sa_scores(b + 2)
                sa_rows(b)
                if b % 2 == 1:
                    ada_reduce(6 + b // 2)
            group(U0["wo_a"], 0, 0, 0, 1)
            group(U0["wo_a"], 1, 1)
            feed_forward(0)

            base = U0["qkv_b"]
            norm(2)
            group(base, 0, 0, 0, 3)
            group(base, 1, 1)
            ada_reduce(18)
            for g in range(2, 4):
                pe.wait_ge(qb_ev, 4 * g - 4)
                group(base, g, g % 2)
                ada_reduce(17 + g)
            for g in range(4, 6):
                pe.wait_ge(qb_ev, 4 * g - 4)
                outs = [(MB[:, 2 * (g % 2) + m, :], True) for m in range(2)]
                for k in range(2):
                    values(base, 2 * g + k, range(4 * k, 4 * k + 4), 0, 512, outs, k == 0, k == 1)
                if g == 4:
                    ada_reduce(21)

            def sb_scores(h):
                t, rows = h // 2, slice(HD * (h % 2), HD * (h % 2) + HD)
                if h >= 4:
                    pe.wait_ge(sb_a, h - 3)
                bank = MB[:, h % 4, :]
                pe.matmul(bank[:, 0:2 * P], KB[rows, t, 0:P], QB[rows, t, :], start=True, stop=False, skip_group_check=True)
                pe.matmul(bank[:, 2 * P:3 * P], KB[rows, t, P:2 * P], QB[rows, t, P:2 * P], start=False, stop=False, skip_group_check=True)
                pe.matmul(bank[:, 0:P], IDB[:, :], MASKB[:, :], start=False, stop=False, skip_group_check=True)
                pe.matmul(bank[:, 2 * P:3 * P], IDB[:, :], MASKB[:, :], start=False, stop=True, skip_group_check=True).then_inc(sb_z, 1)

            def sb_logs(h):
                pe.wait_ge(sb_sp, h + 1)
                bank, sp_ = MB[:, h % 4, :], SP[:, h % 2, :]
                pe.matmul(bank[:, 0:2 * P], TNEG, sp_[:, 0:2 * P], start=False, stop=False, skip_group_check=True)
                pe.matmul(bank[:, P:2 * P], ONEG, sp_[:, 2 * P:3 * P], start=False, stop=False, skip_group_check=True)
                pe.matmul(bank[:, 2 * P:3 * P], TNEG, sp_[:, 2 * P:3 * P], start=False, stop=True, skip_group_check=True).then_inc(sb_e, 1)

            def sb_rows(h):
                t, e = h // 2, h % 2
                if t >= 2:
                    pe.wait_ge(xin_ready, KT * 4 + t - 1)
                pe.wait_ge(sb_a, h + 1)
                o = AUX[HD * e:HD * e + HD, 4 - 4 * (t % 2), :]
                v = slice(HD * h, HD * h + HD)
                pe.matmul(o, VB[:, 0, v], AB[:, h % 2, 0:2 * P], start=True, stop=False, skip_group_check=True)
                pe.matmul(o[:, P:2 * P], VB[:, 1, v], AB[:, h % 2, 2 * P:3 * P], start=False, stop=True, skip_group_check=True).then_inc(sb_o, 1)

            pe.wait_ge(qb_ev, 20)
            for h in range(16 + 2):
                if h < 16:
                    sb_scores(h)
                if 1 <= h <= 16:
                    sb_logs(h - 1)
                if h >= 2:
                    sb_rows(h - 2)
            group(U0["wo_b"], 0, 0, 0, 4)
            group(U0["wo_b"], 1, 1)
            feed_forward(1)

            base = U0["w_in"]
            norm(4)
            group(base, 0, 0, 0, 6)
            pe.wait_ge(mx_tril, 1)
            for h in range(8):
                mm = pe.transpose(AB4[:, h // 4, (h % 4) * P:(h % 4) * P + P], WSP[:, h, :], IDENT)
            mm.then_inc(mx_wt_t, 1)
            group(base, 1, 1)
            ada_reduce(30)
            pe.wait_ge(mx_sg, 4)
            outs = [(MB[:, m, :], True) for m in range(2)]
            for k in range(2):
                values(base, 4 + k, range(4 * k, 4 * k + 4), 0, 512, outs, k == 0, k == 1)
            pe.wait_ge(mx_y0, 4)
            group(base, 3, 1)
            ada_reduce(31)
            pe.wait_ge(mx_wt, 2)
            pe.wait_ge(v_b, 2)
            for j in range(4):
                for e in range(2):
                    h = 2 * j + e
                    for c in range(2):
                        mm = pe.matmul(M[HD * e:HD * e + HD, j, c * P:(c + 1) * P], VN[:, c, HD * h:HD * h + HD], WT[:, h, :],
                                       start=True, stop=True, skip_group_check=True)
                if j % 2 == 1:
                    mm.then_inc(sp_done, 1)
            ada_reduce(32)
            for j in range(4):
                if j == 0:
                    pe.wait_ge(cv_c, 4 * CONV)
                mm = pe.matmul(AUX[:, j, :], BLK, CV[:, j, :], start=True, stop=True)
                if j % 2 == 1:
                    mm.then_inc(gn_mu, 1)

            def out_mean(q):
                if q == 1:
                    pe.wait_ge(on_std, 1)
                for j in range(4):
                    pe.wait_ge(on_sq, 4 * q + j + 1)
                    mm = pe.matmul(AUX[:, 4 + q, :], ONES, TMP[:, 4 * q + j, :], start=(j == 0), stop=(j == 3))
                mm.then_inc(on_ssq, 1)

            out_mean(0)
            ada_reduce(33)
            for j in range(4):
                pe.wait_ge(gn_sq, j + 1)
                pe.wait_ge(gn_c, j + 2 - j % 2)
                mm = pe.matmul(AUX[:, j, :], BLK, TMP[:, 4 + j, :], start=True, stop=True)
                if j % 2 == 1:
                    mm.then_inc(gn_var, 1)
            out_mean(1)
            group(U0["w_out"], 0, 0, 0, 7)
            group(U0["w_out"], 1, 1)
            feed_forward(2)

            norm(6)
            for m in range(2):
                for j in range(KT):
                    if m == 0:
                        pe.wait_ge(xo_ready, j + 1)
                    mm = pe.transpose(M[:, 4 * m + j // 2, (j % 2) * P:(j % 2) * P + P], XO[:, j, m * P:(m + 1) * P], IDENT)
                    if j % 4 == 3:
                        mm.then_inc(o_turned, 1)


_INS = ["x", "c", "positions", "ada_w", "ada_b", "norm1_g", "norm2_g", "wqkv_a", "q_norm_a", "k_norm_a",
        "sinks_a", "wo_a", "wqkv_b", "wo_b", "w_gate", "w_up", "w_down", "c_2", "ada_w_2", "ada_b_2",
        "norm1_g_2", "w_in_2", "b_in_2", "a_ln_g_2", "a_ln_b_2", "a_spatial_w_2", "a_spatial_b_2",
        "b_conv_w_2", "b_conv_b_2", "b_gn_g_2", "b_gn_b_2", "out_norm_a_g_2", "out_norm_b_g_2", "w_out_2",
        "norm2_g_2", "w_ffn_in_2", "w_ffn_out_2", "ada_f_w_2", "ada_f_b_2", "norm_f_g_2"]
_SHORT = {"ada_f_w_2": "ada_f_w", "ada_f_b_2": "ada_f_b", "norm_f_g_2": "norm_f_g"}


def kernel(**inputs):
    import concourse.bacc as bacc
    from concourse.bass_utils import run_bass_kernel_spmd

    nc = bacc.Bacc("TRN2", target_bir_lowering=False, num_devices=1)
    arrays, aps = {}, {}
    kept, temp, tril = constants()
    given = {_SHORT.get(n, n): np.ascontiguousarray(inputs[n]) for n in _INS}
    for name, array in {**given, "kept": kept, "temp": temp, "tril": tril}.items():
        arrays[f"in_{name}"] = array
        aps[name] = nc.dram_tensor(f"in_{name}", array.shape, mybir.dt.from_np(array.dtype), kind="ExternalInput").ap()
    out = nc.dram_tensor("out", (1, T, D), F32, kind="ExternalOutput").ap()
    build(nc, aps, out)
    r = run_bass_kernel_spmd(nc, [arrays], core_ids=[0])
    return r.results[0]["out"]
```

```python
from contextlib import ExitStack

import numpy as np
import concourse.bass as bass
from concourse import mybir

F32 = mybir.dt.float32
F32R = mybir.dt.float32r
BF16 = mybir.dt.bfloat16
I32 = mybir.dt.int32
ALU = mybir.AluOpType
ACT = mybir.ActivationFunctionType
AX_X = mybir.AxisListType.X

P = 128
D = 1024
T = 256
KT = D // P
HD = 64
DFF = 2816
FT = DFF // P
DA = 512
CONV = 31
PE_TAPS = 18
DIAGS = 8
EPS = 1e-6
THETA = 500000.0
ROT = HD // 4
SCALE = HD ** -0.5
NEG = -1e30

UNITS = [("qkv_a", 5), ("wo_a", 4), ("gu0", 22), ("dn0", 11), ("qkv_b", 12), ("wo_b", 4), ("gu1", 22),
         ("dn1", 11), ("w_in", 8), ("w_out", 4), ("gu2", 22), ("dn2", 11)]
BANKS = [("qkv_a", 2), ("wo_a", 2), ("gu0", 11), ("dn0", 3), ("qkv_b", 6), ("wo_b", 2), ("gu1", 11),
         ("dn1", 3), ("w_in", 4), ("w_out", 2), ("gu2", 11), ("dn2", 3)]


def starts(counts):
    at, out = 0, {}
    for name, n in counts:
        out[name] = at
        at += n
    return out


U0 = starts(UNITS)
BD = starts(BANKS)

GU_BLOCKS = [(11, range(6)), (26, range(6)), (35, range(5))]
DN_BLOCKS = [17, 32, None]
QKV_B_BLOCKS = [19, 20, 21, 22]
STICK_BLOCKS = [23, 24, 25]
MIX_BLOCK = 34
MODS_BY_NORM = [4, 10, 16, 22, 28, 34, 40]
MODS_BY_OUT = [6, 18, 30]
MODS_BY_DOWN = [12, 24, 36]

QA_GROUPS = [[0], [1, 2, 3, 4], [5, 6, 7, 8]]
QA_ROWS = [8, 0, 1, 2, 3, 4, 5, 6, 7]
QA_PRODUCT = [0, 4, 5, 6, 7, 0, 1, 2, 3]

ROWS = [("ada_b", 96), ("ada_b_2", 48), ("ada_f_b", 16), ("norm2_g", 16), ("norm1_g_2", 8),
        ("norm2_g_2", 8), ("norm_f_g", 8), ("b_in_2", 16), ("b_conv_b_2", 4), ("b_gn_g_2", 4),
        ("b_gn_b_2", 4), ("out_norm_a_g_2", 4), ("out_norm_b_g_2", 4), ("gap", 20),
        ("norm1_g", 16), ("q_norm_a", 1), ("k_norm_a", 1), ("b_conv_w_2", 4 * CONV)]
COL = starts(ROWS)
N_ROWS = sum(n for _, n in ROWS)
ROW_TILES = -(-N_ROWS // P)
ROWS_IN_TILE = [P, COL["gap"] - P, P, N_ROWS - 3 * P]
EARLY_ROWS, LATE_ROWS = (0, 2), (1, 3)


def row_pieces():
    out = []
    for name, n in ROWS:
        r = 0
        while r < n:
            at = COL[name] + r
            k = min(n - r, P - at % P)
            out.append((name, r, k, at // P, at % P))
            r += k
    return [piece for piece in out if piece[0] != "gap"]


def row_dmas(tiles):
    return sum(2 if name in ("q_norm_a", "k_norm_a") else 1 for name, _, _, tile, _ in row_pieces() if tile in tiles)


KEPT = [("ident", P), ("rot", P), ("blk", P), ("ones", P), ("tneg", P), ("oneg", P), ("cols", 8)]
TEMP = [("swap", P), ("mask_a", 3 * P), ("mask_b", P)]
K0 = starts(KEPT)
K_W = sum(n for _, n in KEPT)
T0 = starts(TEMP)
T_W = sum(n for _, n in TEMP)
C_INVF, C_ROPE, C_KEEP, C_EPS, C_HALFPI, C_ONE = range(6)


def constants():
    k = np.zeros((P, K_W), np.float32)
    t = np.zeros((P, T_W), np.float32)
    tril = np.tril(np.ones((P, P), np.float32))
    i, j = np.arange(P)[:, None], np.arange(P)[None, :]
    k[:, K0["ident"]:K0["ident"] + P] = np.eye(P)
    half = ROT // 2
    rot = np.zeros((P, P), np.float32)
    for base in (0, HD):
        for d in range(half):
            rot[base + d + half, base + d] = -1.0
            rot[base + d, base + d + half] = 1.0
    k[:, K0["rot"]:K0["rot"] + P] = rot
    k[:, K0["blk"]:K0["blk"] + P] = (i // HD == j // HD) / HD
    k[:, K0["ones"]:K0["ones"] + P] = 1.0 / D
    k[:, K0["tneg"]:K0["tneg"] + P] = -(i >= j).astype(np.float32)
    k[:, K0["oneg"]:K0["oneg"] + P] = -1.0
    inv = np.power(np.float32(THETA), -np.arange(half, dtype=np.float32) * np.float32(2.0) / np.float32(ROT))
    c = k[:, K0["cols"]:]
    for base in (0, HD):
        c[base:base + half, C_INVF] = inv
        c[base + half:base + ROT, C_INVF] = inv
        c[base:base + ROT, C_ROPE] = 1.0
    c[:, C_KEEP] = 1.0 - c[:, C_ROPE]
    c[:, C_EPS] = EPS
    c[:, C_HALFPI] = np.pi / 2
    c[:, C_ONE] = 1.0
    t[:, T0["swap"]:T0["swap"] + P] = (i == (j + HD) % P)
    causal = np.where(j > i, NEG, 0.0)
    window = np.where(j <= i, NEG, 0.0)
    t[:, T0["mask_a"]:T0["mask_a"] + 3 * P] = np.concatenate([causal, window, causal], 1)
    t[:, T0["mask_b"]:T0["mask_b"] + P] = np.where(i >= j, NEG, 0.0)
    return k, t, tril


def two_pi_parts():
    parts, left = [], 2 * np.pi
    for bits in (6, 15, 24):
        q = np.floor(left * 2.0 ** bits) / 2.0 ** bits
        parts.append(float(q))
        left -= q
    parts.append(float(np.float32(left)))
    return parts


ROUND = 1.5 * 2.0 ** 23


def build(nc, a, out):
    ctx = ExitStack()
    with ctx:
        def sb(name, shape, dt=F32, stack=ctx):
            return stack.enter_context(nc.sbuf_tensor(name, shape, dt))

        def ps(name, shape):
            return ctx.enter_context(nc.psum_tensor(name, shape, F32))

        def sem(name):
            return ctx.enter_context(nc.semaphore(name))

        RAW = sb("RAW", [P, 4, 2048])
        WH = sb("WH", [P, 4, 2048], F32R)
        WL = sb("WL", [P, 4, 2048], F32R)
        ADA = sb("ADA", [P, 2, 4, 512])
        ACC = sb("ACC", [P, 2, 512])
        X = sb("X", [P, KT, T])
        XH = sb("XH", [P, KT, T], F32R)
        XL = sb("XL", [P, KT, T], F32R)
        TMP = sb("TMP", [P, KT, T])
        CONST = sb("CONST", [P, K_W])
        VC = sb("VC", [P, N_ROWS])
        MOD = sb("MOD", [P, 160])
        COND = sb("COND", [P, 2 * KT])
        COEF = sb("COEF", [P, KT])
        STD = sb("STD", [P, 2])
        RSTD = sb("RSTD", [P, 2])
        IDB = sb("IDB", [P, P], BF16)
        MASKA = sb("MASKA", [P, 3 * P], BF16)
        MASKB = sb("MASKB", [P, P], BF16)

        s1 = ExitStack()
        with s1:
            VROWS = sb("VROWS", [P, ROW_TILES, P], F32, s1)
            CROWS = sb("CROWS", [2 * KT, P], F32, s1)
            CTMP = sb("CTMP", [P, T_W], F32, s1)
            POSI = sb("POSI", [P, T], I32, s1)
            ANG = sb("ANG", [P, 4, T], F32, s1)
            COS = sb("COS", [P, T], F32, s1)
            SIN = sb("SIN", [P, T], F32, s1)
            SINK = sb("SINK", [P, 2, 16], F32, s1)
            NSINK = sb("NSINK", [P, 2, 16], F32, s1)
            with ExitStack() as s0:
                ADA3 = sb("ADA3", [P, KT, 512], F32, s0)
            QA = sb("QA", [P, 9, T], F32, s1)
            KS = sb("KS", [P, T], F32, s1)
            VTURN = sb("VTURN", [P, T], F32, s1)
            VA = sb("VA", [P, 2, P], F32, s1)
            QSQ = sb("QSQ", [P, 2, T], F32, s1)
            QSTD = sb("QSTD", [P, 3, 16], F32, s1)
            QRS = sb("QRS", [P, 3, 16], F32, s1)
            QN = sb("QN", [P, 4, T], F32, s1)
            QT2 = sb("QT2", [P, 2, T], F32, s1)
            PR = sb("PR", [P, 2, 2, 384], F32, s1)
            PT = sb("PT", [P, 2, 2, 384], F32, s1)
            SM = sb("SM", [P, 2, 6, 4], F32, s1)
            RS_SUM = sb("RS_SUM", [P, 2, 4], F32, s1)
        s2 = ExitStack()
        with s2:
            QB = sb("QB", [P, KT, T], F32, s2)
            KB = sb("KB", [P, KT, T], F32, s2)
            VB = sb("VB", [P, 2, D], F32, s2)
            ZP = sb("ZP", [P, 3, 384], F32, s2)
            AZ = sb("AZ", [P, 3, 384], F32, s2)
            SP = sb("SP", [P, 3, 384], F32, s2)
            AB = sb("AB", [P, 2, 384], F32, s2)
        s3 = ExitStack()
        with s3:
            WSP = sb("WSP", [P, 8, P], F32, s3)
            TRIL = sb("TRIL", [P, P], F32, s3)
            WT = sb("WT", [P, 8, P], F32, s3)
            BSB = sb("BSB", [P, 4, P], F32, s3)
            LNG = sb("LNG", [P, DA], F32, s3)
            LNB = sb("LNB", [P, DA], F32, s3)
            BV = sb("BV", [P, DA], F32, s3)
            SG = sb("SG", [P, 4, T], F32, s3)
            Y0 = sb("Y0", [P, 4, CONV - 1 + T], F32, s3)
            CV = sb("CV", [P, 4, T], F32, s3)
            UG = sb("UG", [P, 4, T], F32, s3)
            VX = sb("VX", [P, 2, DA], F32, s3)
            VN = sb("VN", [P, 2, DA], F32, s3)
            VST = sb("VST", [P, 2, 8], F32, s3)
            GSTD = sb("GSTD", [P, 16], F32, s3)
            GRS = sb("GRS", [P, 16], F32, s3)
        s4 = ExitStack()
        with s4:
            XO = sb("XO", [P, KT, T], F32, s4)
            OUT = sb("OUT", [P, 2, D], F32, s4)
        MH = sb("MH", [P, FT, T], F32R)
        ML = sb("ML", [P, FT, T], F32R)
        MHF, MLF = (m[:, :, :].rearrange("p f t -> p (f t)") for m in (MH, ML))

        EARLY = [ADA[:, :, :, :].rearrange("p h t n -> p (h t) n")] + [
            RAW[:, s0:s0 + 2, :].rearrange("p s (t n) -> p (s t) n", n=512) for s0 in (0, 2)] + [ADA3[:, :, :]]

        M = ps("M", [P, 8, T])
        AUX = ps("AUX", [P, 8, T])
        MB = M[:, :, :].rearrange("p (b h) t -> p b (h t)", h=2)
        AB4 = AUX[:, :, :].rearrange("p (b h) t -> p b (h t)", h=2)
        ADP = AUX[:, 6, 0:4]
        ON_SUMS = [M[:, 1, 0:2], AUX[:, 5, 32:34]]
        ON_SPREAD = [M[:, 0, :], AUX[:, 4, :]]

        def kc(name, n=P):
            return CONST[:, K0[name]:K0[name] + n]

        def cc(i):
            return CONST[:, K0["cols"] + i:K0["cols"] + i + 1]

        def vc(name, i, n=1):
            return VC[:, COL[name] + i:COL[name] + i + n]

        def mod(layer, chunk, i, n=1):
            at = layer * 48 + chunk * 8 + i
            return MOD[:, at:at + n]

        IDENT, ROTM, BLK, ONES, TNEG, ONEG = (kc(n) for n in ("ident", "rot", "blk", "ones", "tneg", "oneg"))
        XTOK = TMP[:, :, :].rearrange("p (m a) t -> p m (a t)", m=2)

        landed = [sem(f"landed{i}") for i in range(4)]
        h_ready, l_ready, w_used, bank_done = sem("h_ready"), sem("l_ready"), sem("w_used"), sem("bank_done")
        a_landed = [sem(f"a_landed{i}") for i in range(2)]
        early_landed = [[sem(f"early_landed{i}_{h}") for h in range(2)] for i in range(len(EARLY))]
        a_chain, acc_red, mod_ready = sem("a_chain"), sem("acc_red"), sem("mod_ready")
        x_ready, sq_ready, ssq_ready, std_ready = sem("x_ready"), sem("sq_ready"), sem("ssq_ready"), sem("std_ready")
        rstd_ready, rstd_spread, coef_ready, t_ready = (sem(n) for n in ("rstd_ready", "rstd_spread", "coef_ready", "t_ready"))
        hh_ready, xin_ready = sem("hh_ready"), sem("xin_ready")
        silu_ready, midf_ready, midh_ready, mid_ready = (sem(n) for n in ("silu_ready", "midf_ready", "midh_ready", "mid_ready"))
        crows_in, const_in, early_rows_in, late_rows_in, x_in, pos_in, misc_in = (
            sem(n) for n in ("crows_in", "const_in", "early_rows_in", "late_rows_in", "x_in", "pos_in", "misc_in"))
        c_turned, cond_ready, rows_turned, vc_ready, x_turned = (sem(n) for n in ("c_turned", "cond_ready", "rows_turned", "vc_ready", "x_turned"))
        masks_ready, ang_v, ang_s, trig_ready, sink_ready, gain_ready = (
            sem(n) for n in ("masks_ready", "ang_v", "ang_s", "trig_ready", "sink_ready", "gain_ready"))
        qa_sq, qa_gain, qa_ssq, qa_std, qa_rs, qa_spread, qa_n, qa_rot, qa_c, qa_t2, qa_q, ks_t, ks_ready, v_turn, v_turned, va_ready = (
            sem(n) for n in ("qa_sq", "qa_gain", "qa_ssq", "qa_std", "qa_rs", "qa_spread", "qa_n", "qa_rot", "qa_c", "qa_t2", "qa_q", "ks_t", "ks_ready", "v_turn", "v_turned", "va_ready"))
        sa_s, sa_m, sa_mr, sa_nm, sa_d, sa_p, sa_e, sa_t, sa_r, sa_pn, sa_tr, sa_ptc, sa_o = (
            sem(n) for n in ("sa_s", "sa_m", "sa_mr", "sa_nm", "sa_d", "sa_p", "sa_e", "sa_t", "sa_r", "sa_pn", "sa_tr", "sa_ptc", "sa_o"))
        qb_ev, sb_z, sb_zp, sb_az, sb_ex, sb_ln, sb_sp, sb_e, sb_a, sb_o = (
            sem(n) for n in ("qb_ev", "sb_z", "sb_zp", "sb_az", "sb_ex", "sb_ln", "sb_sp", "sb_e", "sb_a", "sb_o"))
        mx_in, mx_tril, mx_wt_t, mx_wt, mx_pad, mx_sg, mx_y0, cv_c, dg_ready, dg_used, cv_ready, ug_ready = (
            sem(n) for n in ("mx_in", "mx_tril", "mx_wt_t", "mx_wt", "mx_pad", "mx_sg", "mx_y0", "cv_c", "dg_ready", "dg_used", "cv_ready", "ug_ready"))
        v_x, v_g, v_mu, v_c, v_s2, v_sd, v_rs, v_n, v_b = (sem(n) for n in ("v_x", "v_g", "v_mu", "v_c", "v_s2", "v_sd", "v_rs", "v_n", "v_b"))
        gn_mu, gn_c, gn_sq, gn_var, gn_std, gn_rs, gn_spread, gn_n, yb_ready = (
            sem(n) for n in ("gn_mu", "gn_c", "gn_sq", "gn_var", "gn_std", "gn_rs", "gn_spread", "gn_n", "yb_ready"))
        sp_done, ya_t, ya_ready = sem("sp_done"), sem("ya_t"), sem("ya_ready")
        on_sq, on_ssq, on_std, on_rs, on_spread, on_t = (sem(n) for n in ("on_sq", "on_ssq", "on_std", "on_rs", "on_spread", "on_t"))
        xo_ready, o_turned, o_copied, o_stored = (sem(n) for n in ("xo_ready", "o_turned", "o_copied", "o_stored"))

        def kp(w):
            return w.rearrange("(t p) n -> p t n", p=P)

        ada_src = [kp(a["ada_w"][0]), kp(a["ada_w"][1]), kp(a["ada_w_2"][0]), kp(a["ada_f_w"])]
        gate_src = [kp(a["w_gate"][0]), kp(a["w_gate"][1]), kp(a["w_ffn_in_2"][0])[:, :, 0:DFF]]
        up_src = [kp(a["w_up"][0]), kp(a["w_up"][1]), kp(a["w_ffn_in_2"][0])[:, :, DFF:2 * DFF]]
        down_src = [kp(a["w_down"][0]), kp(a["w_down"][1]), kp(a["w_ffn_out_2"][0])]
        qkv_a_src, wo_a_src = kp(a["wqkv_a"][0]), kp(a["wo_a"][0])
        qkv_b_src, wo_b_src = kp(a["wqkv_b"][0]), kp(a["wo_b"][0])
        in_src, out_src = kp(a["w_in_2"][0]), kp(a["w_out_2"][0])
        IN_COLS = [3 * DA, 2 * DA, DA, 0]

        def slot(base, k):
            return (base + k) % 4

        def landed_by(base, k, i):
            return 32 * ((base + k) // 4 + 1) + 32 * i

        def acc_slot(b):
            return b % 2 if b < len(EARLY) else 0

        def load_rows(engine, tiles, loaded):
            for name, r, n, tile, at in row_pieces():
                if tile not in tiles:
                    continue
                src = a[name]
                if name in ("q_norm_a", "k_norm_a"):
                    for h in range(2):
                        engine.dma_start(VROWS[at:at + 1, tile, HD * h:HD * h + HD], src).then_inc(loaded, 16)
                    continue
                if name == "ada_f_b" or name == "norm_f_g":
                    view = src.rearrange("(t p) -> t p", p=P)
                elif name == "b_conv_w_2":
                    view = src[0].rearrange("k (j p) -> (k j) p", p=P)
                else:
                    view = src.rearrange("l (t p) -> (l t) p", p=P)
                engine.dma_start(VROWS[at:at + n, tile, :], view[r:r + n, :]).then_inc(loaded, 16)

        block = ctx.enter_context(nc.Block())

        @block.sync
        def _(sp):
            sp.dma_start(CROWS[0:KT, :], a["c"].rearrange("a (t p) -> (a t) p", p=P)).then_inc(crows_in, 16)
            sp.dma_start(CROWS[KT:2 * KT, :], a["c_2"].rearrange("a (t p) -> (a t) p", p=P)).then_inc(crows_in, 16)
            load_rows(sp, EARLY_ROWS, early_rows_in)

            def ada_load(src, col, b, i=0, halves=(0, 1)):
                if not isinstance(col, int):
                    col = sp.snap(col)
                for h in halves:
                    if b == len(EARLY):
                        sp.wait_ge(a_chain, 4 * h + 4)
                    else:
                        sp.wait_ge(a_chain, 8 * b + 4 * h - 4 + 8 * i)
                    sp.dma_start(ADA[:, h, :, :], src[:, 4 * h:4 * h + 4, bass.ds(col, 512)]).then_inc(a_landed[h], 16)

            def ada_block(b):
                ada_load(ada_src[b // 12], 512 * (b % 12), b)

            def unit_free(base, k, i=0):
                if base + k >= 4:
                    sp.wait_ge(l_ready, base + k - 3 + 4 * i)
                else:
                    sp.wait_ge(a_chain, KT * (2 + k // 2))

            def load_square(base, k, src, col, half=None):
                unit_free(base, k)
                s, t0 = slot(base, k), 4 * (k % 2 if half is None else half)
                for q in range(2):
                    sp.dma_start(RAW[:, s, 1024 * q:1024 * q + 1024].rearrange("p (t n) -> p t n", t=2),
                                 src[:, t0 + 2 * q:t0 + 2 * q + 2, col:col + 512]).then_inc(landed[s], 16)

            def load_gate_up(layer, base, k, col, i=0):
                unit_free(base, k, i)
                s, t0 = slot(base, k), 4 * (k % 2)
                view = RAW[:, s, :].rearrange("p (t n) -> p t n", t=4)
                sp.dma_start(view[:, :, 0:256], gate_src[layer][:, t0:t0 + 4, bass.ds(col, 256)]).then_inc(landed[s], 16)
                sp.dma_start(view[:, :, 256:512], up_src[layer][:, t0:t0 + 4, bass.ds(col, 256)]).then_inc(landed[s], 16)

            def load_down(layer, base, k, row, i=0):
                rows = [row, row + 1]
                unit_free(base, k, i)
                s = slot(base, k)
                for q in range(2):
                    sp.dma_start(RAW[:, s, 1024 * q:1024 * q + 1024].rearrange("p (t n) -> p t n", t=1),
                                 down_src[layer][:, bass.ds(rows[q], 1), :]).then_inc(landed[s], 16)

            def feed_forward(layer):
                base, (b0, steps) = U0[f"gu{layer}"], GU_BLOCKS[layer]

                def step(i, before, first):
                    b = b0 + before
                    for k in range(4):
                        load_gate_up(layer, base + 4 * before, k, i * 512 + (512 * before + 256 * (k // 2)), i)
                        if k % 2 == 1:
                            col = i * 512 + 512 * (first % 12 + b - first)
                            ada_load(ada_src[first // 12], col, b, i, (k // 2,))

                step(0, 0, b0)
                before = 0 if layer == 2 else 1
                with sp.Fori(1 - before, 5 - before) as i:
                    step(i, before, b0 + 1)
                for k in range(2):
                    load_gate_up(layer, base + 20, k, 5 * 512)
                base, b0 = U0[f"dn{layer}"], DN_BLOCKS[layer]
                for k in range(2):
                    load_down(layer, base, k, 2 * k)
                if 5 in steps:
                    ada_block(GU_BLOCKS[layer][0] + 5)
                with sp.Fori(0, 2) as i:
                    for k in range(2, 6):
                        load_down(layer, base, k, i * 8 + 2 * k, i)
                        if k == 3 and b0 is not None:
                            ada_load(ada_src[b0 // 12], i * 512 + 512 * (b0 % 12), b0, i)
                load_down(layer, base, 10, 20)

            for b in range(len(EARLY)):
                for h in range(2):
                    sp.dma_start(EARLY[b][:, 4 * h:4 * h + 4, :],
                                 ada_src[0][:, 4 * h:4 * h + 4, 512 * b:512 * b + 512]).then_inc(early_landed[b][h], 16)
                if b == 0:
                    sp.dma_start(XTOK, a["x"][0].rearrange("(m p) d -> p m d", p=P)).then_inc(x_in, 16)
            unit_free(U0["qkv_a"], 0)
            for q in range(2):
                sp.dma_start(RAW[:, 0, 1024 * q:1024 * q + 1024].rearrange("p (t n) -> p t n", t=4),
                             qkv_a_src[:, 4 * q:4 * q + 4, D:D + 256]).then_inc(landed[0], 16)
            for k in range(3):
                load_square(U0["qkv_a"], 1 + k, qkv_a_src, 512 * (k // 2), k % 2)
            ada_block(4)
            load_square(U0["qkv_a"], 4, qkv_a_src, 512, 1)
            for k in range(3):
                load_square(U0["wo_a"], k, wo_a_src, 512 * (k // 2))
            ada_block(5)
            load_square(U0["wo_a"], 3, wo_a_src, 512)
            for b in range(6, 11):
                ada_block(b)
            feed_forward(0)

            for g in range(6):
                if g in (1, 4, 5):
                    ada_block(QKV_B_BLOCKS[(1, 4, 5).index(g)])
                for k in range(2):
                    load_square(U0["qkv_b"], 2 * g + k, qkv_b_src, 512 * g)
            ada_block(QKV_B_BLOCKS[3])
            for k in range(4):
                load_square(U0["wo_b"], k, wo_b_src, 512 * (k // 2))
            for b in STICK_BLOCKS:
                ada_block(b)
            feed_forward(1)

            for g in range(4):
                if g == 3:
                    ada_block(MIX_BLOCK)
                for k in range(2):
                    load_square(U0["w_in"], 2 * g + k, in_src, IN_COLS[g])
            for k in range(4):
                load_square(U0["w_out"], k, out_src, 512 * (k % 2), 1 - k // 2)
            feed_forward(2)

            for m in range(2):
                sp.wait_ge(o_copied, 2 * m + 2)
                sp.dma_start(out[0, m * P:(m + 1) * P, :], OUT[:, m, :]).then_inc(o_stored, 16)
            sp.wait_ge(o_stored, 32)

        @block.gpsimd
        def _(pool):
            pool.wait_ge(x_in, 16)
            pool.dma_start(CTMP[:, :], a["temp"]).then_inc(misc_in, 16)
            for h in range(2):
                pool.dma_start(SINK[:, h, :], a["sinks_a"][0].partition_broadcast(P)).then_inc(misc_in, 16)
            load_rows(pool, LATE_ROWS, late_rows_in)
            pool.wait_ge(w_used, U0["w_in"])
            pool.dma_start(WSP[:, :, :], a["a_spatial_w_2"][0].rearrange("h t s -> t h s")).then_inc(mx_in, 16)
            pool.dma_start(TRIL[:, :], a["tril"]).then_inc(mx_in, 16)
            for e in range(2):
                pool.dma_start(BSB[HD * e:HD * e + HD, :, :],
                               a["a_spatial_b_2"][0].rearrange("(j e) t -> e j t", e=2)[e].partition_broadcast(HD)).then_inc(mx_in, 16)
            pool.dma_start(LNG[:, :], a["a_ln_g_2"][0].partition_broadcast(P)).then_inc(mx_in, 16)
            pool.dma_start(LNB[:, :], a["a_ln_b_2"][0].partition_broadcast(P)).then_inc(mx_in, 16)
            pool.dma_start(BV[:, :], a["b_in_2"][0, DA:2 * DA].partition_broadcast(P)).then_inc(mx_in, 16)

        @block.scalar
        def _(act):
            act.dma_start(CONST[:, :], a["kept"]).then_inc(const_in, 16)
            act.dma_start(POSI[:, :], a["positions"][0].partition_broadcast(P)).then_inc(pos_in, 16)

            def high(base, k, i=0):
                s = slot(base, k)
                act.wait_ge(landed[s], landed_by(base, k, i))
                if base + k >= 4:
                    act.wait_ge(w_used, base + k - 3 + 4 * i)
                act.activation(WH[:, s, :], RAW[:, s, :], ACT.Copy).then_inc(h_ready, 1)

            def wait_tile(stage, group, n, last_unit):
                if n < 2:
                    act.wait_ge(bank_done, BD[stage] + group + 1)
                else:
                    act.wait_ge(w_used, last_unit + 1)

            def norm(n, before=None):
                act.preload_act_table(ACT.Sqrt)
                for j in range(KT):
                    act.wait_ge(x_ready, KT * n + j + 1)
                    act.activation(TMP[:, j, :], X[:, j, :], ACT.Square).then_inc(sq_ready, 1)
                act.wait_ge(ssq_ready, n + 1)
                act.activation(STD[:, :], AUX[:, 0, 0:2], ACT.Sqrt, bias=cc(C_EPS)).then_inc(std_ready, 1)
                if before is not None:
                    before()
                for j in range(KT):
                    act.wait_ge(t_ready, KT * n + j + 1)
                    shift = mod(n // 2, 3 * (n % 2), j)
                    if n == 6:
                        act.activation(XO[:, j, :], TMP[:, j, :], ACT.Identity, bias=shift).then_inc(xo_ready, 1)
                    else:
                        act.activation(XH[:, j, :], TMP[:, j, :], ACT.Identity, bias=shift).then_inc(hh_ready, 1)

            def feed_forward(layer):
                base, m0, td = U0[f"gu{layer}"], FT * layer, BD[f"gu{layer}"]

                def gates(i, g):
                    for n in range(2):
                        act.wait_ge(bank_done, i * 2 + td + g + 1)
                        act.activation(TMP[:, 2 * g + n, :], M[:, 4 * g + n, :], ACT.Silu).then_inc(silu_ready, 1)

                def product_highs(i, g):
                    for n in range(2):
                        act.wait_ge(midf_ready, i * 4 + m0 + 2 * g + n + 1)
                        act.activation(MHF[:, bass.ds((i * 4 + 2 * g + n) * T, T)], TMP[:, 4 + 2 * g + n, :], ACT.Copy).then_inc(midh_ready, 1)

                high(base, 0)
                high(base, 1)
                norm(2 * layer + 1)
                act.preload_act_table(ACT.Silu)
                high(base, 2)
                high(base, 3)
                with act.Fori(1, 5) as i:
                    high(base, 0, i)
                    high(base, 1, i)
                    gates(i - 1, 0)
                    product_highs(i - 1, 0)
                    high(base, 2, i)
                    gates(i - 1, 1)
                    high(base, 3, i)
                    product_highs(i - 1, 1)
                high(base, 20)
                high(base, 21)
                gates(4, 0)
                product_highs(4, 0)
                base = U0[f"dn{layer}"]
                high(base, 0)
                gates(4, 1)
                high(base, 1)
                product_highs(4, 1)
                gates(5, 0)
                product_highs(5, 0)
                with act.Fori(0, 2) as i:
                    for k in range(2, 6):
                        high(base, k, i)
                high(base, 10)

            act.wait_ge(c_turned, 1)
            act.activation(COND[:, :], AUX[:, 0, 0:2 * KT], ACT.Silu).then_inc(cond_ready, 1)

            def columns(tiles):
                for r in tiles:
                    n = ROWS_IN_TILE[r]
                    turned = AUX[:, 2 + r // 2, (r % 2) * P:(r % 2) * P + n]
                    act.activation(VC[:, r * P:r * P + n], turned, ACT.Copy).then_inc(vc_ready, 1)

            act.wait_ge(rows_turned, 1)
            columns(EARLY_ROWS)
            for j in range(KT):
                act.wait_ge(x_turned, j // 2 + 1)
                act.activation(X[:, j, :], M[:, j, :], ACT.Copy).then_inc(x_ready, 1)
            act.wait_ge(ang_v, 10)
            act.activation(SIN[:, :], ANG[:, 0, :], ACT.Sin).then_inc(ang_s, 1)
            act.activation(COS[:, :], ANG[:, 1, :], ACT.Sin, bias=cc(C_HALFPI)).then_inc(ang_s, 1)
            norm(0, before=lambda: high(U0["qkv_a"], 0))
            for k in range(1, 4):
                high(U0["qkv_a"], k)

            def qa_take(i):
                if i == 0:
                    act.wait_ge(w_used, 1)
                else:
                    wait_tile("qkv_a", (i - 1) // 4, (i - 1) % 4, 2 * ((i - 1) // 4) + 2)
                if i >= 2:
                    act.wait_ge(qa_ssq, i - 1)
                act.activation(QSQ[:, i % 2, :], M[:, QA_PRODUCT[i], :], ACT.Square).then_inc(qa_sq, 1)
                if i >= 4:
                    act.wait_ge(qa_rot, i - 3)
                    act.wait_ge(qa_c, i - 3)
                rows = QA[:, 8, :] if i == 0 else QN[:, i % 4, :]
                gain = vc("k_norm_a" if i == 0 else "q_norm_a", 0)
                act.activation(rows, M[:, QA_PRODUCT[i], :], ACT.Copy, scale=gain).then_inc(qa_gain, 1)

            def qa_roots(g):
                n = len(QA_GROUPS[g])
                act.wait_ge(qa_ssq, QA_GROUPS[g][-1] + 1)
                act.activation(QSTD[:, g, 0:4 * n], AUX[:, 2 * (g % 2), 0:4 * n], ACT.Sqrt, bias=cc(C_EPS)).then_inc(qa_std, 1)

            act.wait_ge(gain_ready, 1)
            qa_take(0)
            act.activation(VTURN[:, :], M[:, 1, :], ACT.Copy).then_inc(v_turn, 1)
            qa_roots(0)
            act.wait_ge(v_turned, 1)
            act.activation(VA[:, :, :], M[:, 1, :].rearrange("p (m d) -> p m d", m=2), ACT.Copy).then_inc(va_ready, 1)
            act.wait_ge(rows_turned, 2)
            columns(LATE_ROWS)
            high(U0["qkv_a"], 4)
            act.wait_ge(ks_t, 1)
            act.activation(KS[:, :], AUX[:, 4, :], ACT.Copy).then_inc(ks_ready, 1)
            for i in range(1, 5):
                qa_take(i)
            qa_roots(1)
            high(U0["wo_a"], 0)
            for i in range(5, 9):
                qa_take(i)
            qa_roots(2)
            act.preload_act_table(ACT.Exp)

            def sa_exp(b):
                act.wait_ge(sa_nm, b + 1)
                if b >= 2:
                    act.wait_ge(sa_tr, 2 * (b - 1))
                for e in range(2):
                    for blk, lo, hi in ((0, 0, P), (1, P, 3 * P)):
                        root = 4 * (b % 4) + 2 * blk + e
                        act.activation(PR[:, b % 2, e, lo:hi], MB[:, 2 - 2 * (b % 2) + e, lo:hi], ACT.Exp,
                                       scale=QRS[:, 1 + b // 4, root:root + 1],
                                       bias=SM[:, b % 2, 1, 2 * e + blk:2 * e + blk + 1],
                                       accum_out=RS_SUM[:, b % 2, 2 * e + blk:2 * e + blk + 1]).then_inc(sa_p, 1)
                act.wait_ge(sa_d, b + 1)
                act.activation(SM[:, b % 2, 3, :], SM[:, b % 2, 2, :], ACT.Exp).then_inc(sa_e, 1)

            def sa_divide(b):
                act.wait_ge(sa_r, b + 1)
                p = b % 2
                for e in range(2):
                    for blk, lo, hi in ((0, 0, P), (1, P, 3 * P)):
                        act.activation(PR[:, p, e, lo:hi], PR[:, p, e, lo:hi], ACT.Copy,
                                       scale=SM[:, p, 5, 2 * e + blk:2 * e + blk + 1]).then_inc(sa_pn, 1)

            sa_exp(0)
            sa_divide(0)
            sa_exp(1)
            for b in range(8):
                for e in range(2):
                    act.wait_ge(sa_tr, 2 * b + e + 1)
                    if b >= 2:
                        act.wait_ge(sa_o, b - 1)
                    act.activation(PT[:, b % 2, e, :], AB4[:, e, 0:384], ACT.Copy).then_inc(sa_ptc, 1)
                if b + 1 < 8:
                    sa_divide(b + 1)
                if b + 2 < 8:
                    sa_exp(b + 2)
                act.wait_ge(sa_o, b + 1)
                act.activation(XH[:, b, :], AUX[:, 4, :], ACT.Copy).then_inc(hh_ready, 1)
                if b in (1, 3, 5):
                    high(U0["wo_a"], (b + 1) // 2)
            feed_forward(0)

            base = U0["qkv_b"]

            def qb_copy(g):
                if g < 4:
                    dst = QB if g < 2 else KB
                    for n in range(4):
                        wait_tile("qkv_b", g, n, base + 2 * g + 1)
                        act.activation(dst[:, 4 * (g % 2) + n, :], M[:, 4 * (g % 2) + n, :], ACT.Copy,
                                       scale=SCALE if g < 2 else 1.0).then_inc(qb_ev, 1)
                else:
                    for m in range(2):
                        if m == 0:
                            act.wait_ge(bank_done, BD["qkv_b"] + g + 1)
                        else:
                            act.wait_ge(w_used, base + 2 * g + 2)
                        act.activation(VB[:, m, 512 * (g - 4):512 * (g - 4) + 512], MB[:, 2 * (g % 2) + m, :], ACT.Copy).then_inc(qb_ev, 1)

            high(base, 0)
            high(base, 1)
            norm(2)
            high(base, 2)
            high(base, 3)
            for g in range(2, 6):
                high(base, 2 * g)
                high(base, 2 * g + 1)
                qb_copy(g - 2)
            for k in range(2):
                high(U0["wo_b"], k)
            qb_copy(4)
            for k in range(2, 4):
                high(U0["wo_b"], k)
            qb_copy(5)

            def sb_softplus(h):
                act.wait_ge(sb_az, h + 1)
                act.activation(AZ[:, h % 3, :], AZ[:, h % 3, :], ACT.Exp).then_inc(sb_ex, 1)
                act.wait_ge(sb_ex, h + 1)
                act.activation(AZ[:, h % 3, :], AZ[:, h % 3, :], ACT.Ln, bias=cc(C_ONE)).then_inc(sb_ln, 1)

            def sb_weights(h):
                act.wait_ge(sb_e, h + 1)
                if h >= 2:
                    act.wait_ge(sb_o, h - 1)
                act.activation(AB[:, h % 2, :], MB[:, h % 4, 0:384], ACT.Exp).then_inc(sb_a, 1)

            def sb_high(t):
                act.wait_ge(sb_o, 2 * t + 2)
                act.activation(XH[:, t, :], AUX[:, 4 - 4 * (t % 2), :], ACT.Copy).then_inc(hh_ready, 1)

            act.preload_act_table_set("natural_log_exp_and_others")
            sb_softplus(0)
            sb_softplus(1)
            for h in range(16):
                if h + 2 < 16:
                    sb_softplus(h + 2)
                sb_weights(h)
                if h >= 2 and h % 2 == 0:
                    sb_high((h - 2) // 2)
            sb_high(7)
            feed_forward(1)

            base = U0["w_in"]
            high(base, 0)
            high(base, 1)
            norm(4)
            high(base, 2)
            high(base, 3)
            act.preload_act_table(ACT.Sigmoid)
            act.wait_ge(mx_wt_t, 1)
            for q in range(2):
                act.activation(WT[:, 4 * q:4 * q + 4, :], AB4[:, q, :].rearrange("p (h t) -> p h t", h=4), ACT.Copy).then_inc(mx_wt, 1)

            def diagonal(k, slot_, i=0):
                w = COL["b_conv_w_2"] + slot_ % 4
                act.activation(WSP[:, slot_, :], IDENT, ACT.Copy, scale=VC[:, bass.ds(k * 4 + w, 1)]).then_inc(dg_ready, 1)

            for q in range(DIAGS):
                diagonal(q // 4, q)
            high(base, 4)
            high(base, 5)
            for j in range(4):
                wait_tile("w_in", 0, j, base + 1)
                act.activation(SG[:, j, :], M[:, j, :], ACT.Sigmoid, bias=vc("b_in_2", 12 + j)).then_inc(mx_sg, 1)
            high(base, 6)
            high(base, 7)
            with act.Fori(1, PE_TAPS // 2) as i:
                for q in range(DIAGS):
                    act.wait_ge(dg_used, i * DIAGS + (q - DIAGS + 1))
                    diagonal(i * 2 + q // 4, q)
            act.preload_act_table(ACT.Sqrt)
            for j in range(4):
                act.wait_ge(gn_c, j + 1)
                act.activation(TMP[:, 4 + j, :], CV[:, j, :], ACT.Square).then_inc(gn_sq, 1)
            act.wait_ge(gn_var, 1)
            act.activation(GSTD[:, :], AUX[:, 5, 0:16], ACT.Sqrt, bias=cc(C_EPS)).then_inc(gn_std, 1)
            act.preload_act_table(ACT.Gelu)
            high(U0["w_out"], 0)
            for m in range(2):
                act.wait_ge(v_x, m + 1)
                act.activation(VN[:, m, :], VX[:, m, :], ACT.Gelu, accum_out=VST[:, m, 0:1]).then_inc(v_g, 1)
            high(U0["w_out"], 1)
            for m in range(2):
                act.wait_ge(v_c, m + 1)
                act.activation(VN[:, m, :], VX[:, m, :], ACT.Square, accum_out=VST[:, m, 2:3]).then_inc(v_s2, 1)
            for m in range(2):
                act.wait_ge(v_s2, m + 1)
                act.activation(VST[:, m, 3:4], VST[:, m, 2:3], ACT.Sqrt, scale=1.0 / DA, bias=cc(C_EPS)).then_inc(v_sd, 1)
            for j in range(4):
                act.wait_ge(gn_n, j + 1)
                act.activation(SG[:, j, :], CV[:, j, :], ACT.Silu, scale=vc("b_gn_g_2", j), bias=vc("b_gn_b_2", j)).then_inc(yb_ready, 1)
            for j in range(4):
                act.wait_ge(yb_ready, j + 1)
                act.activation(TMP[:, 4 + j, :], SG[:, j, :], ACT.Square).then_inc(on_sq, 1)
            for j in range(4):
                wait_tile("w_in", 3, j, base + 7)
                act.activation(UG[:, j, :], M[:, 4 + j, :], ACT.Gelu, bias=vc("b_in_2", j)).then_inc(ug_ready, 1)

            def out_norm(turn):
                q = 1 - turn
                act.wait_ge(on_ssq, turn + 1)
                if turn == 1:
                    act.wait_ge(on_rs, 1)
                act.activation(STD[:, :], ON_SUMS[turn], ACT.Sqrt, scale=float(D // DA), bias=cc(C_EPS)).then_inc(on_std, 1)
                for j in range(4):
                    act.wait_ge(on_t, 4 * turn + j + 1)
                    act.activation(XH[:, 4 * q + j, :], TMP[:, 4 * q + j, :], ACT.Copy).then_inc(hh_ready, 1)

            out_norm(0)
            high(U0["w_out"], 2)
            high(U0["w_out"], 3)
            for j in range(4):
                act.wait_ge(ya_ready, j + 1)
                act.activation(TMP[:, j, :], UG[:, j, :], ACT.Square).then_inc(on_sq, 1)
            out_norm(1)
            feed_forward(2)

            norm(6)
            for q in range(4):
                act.wait_ge(o_turned, q + 1)
                act.activation(OUT[:, q // 2, 512 * (q % 2):512 * (q % 2) + 512], MB[:, q, :], ACT.Copy).then_inc(o_copied, 1)

        @block.vector
        def _(dve):
            GAINS = [("norm1_g", 0), ("norm2_g", 0), ("norm1_g", 8), ("norm2_g", 8), ("norm1_g_2", 0),
                     ("norm2_g_2", 0), ("norm_f_g", 0)]

            def low(base, k, i=0):
                s = slot(base, k)
                dve.wait_ge(h_ready, base + k + 1 + 4 * i)
                dve.tensor_tensor(WL[:, s, :], RAW[:, s, :], WH[:, s, :], ALU.subtract).then_inc(l_ready, 1)

            def ada_sum(b, second, i=0, rows=range(KT)):
                for kt in rows:
                    w = EARLY[b if b < len(EARLY) else 0][:, kt, :]
                    scale = COND[:, KT * second + kt:KT * second + kt + 1]
                    if b < len(EARLY):
                        if kt % 4 == 0:
                            dve.wait_ge(early_landed[b][kt // 4], 16)
                    elif kt % 4 == 0:
                        dve.wait_ge(a_landed[kt // 4], 16 * (b + 1 - len(EARLY)) + 16 * i)
                    acc = ACC[:, acc_slot(b), :]
                    if kt == 0 and b >= len(EARLY):
                        dve.wait_ge(acc_red, b + i)
                    elif kt == 0 and b >= 2:
                        dve.wait_ge(acc_red, b - 1)
                    if kt == 0:
                        dve.tensor_scalar(acc, w, scale, None, ALU.mult).then_inc(a_chain, 1)
                    else:
                        dve.wait_ge(a_chain, 8 * b + kt + 8 * i)
                        dve.scalar_tensor_tensor(out=acc, in0=w, scalar=scale, in1=acc,
                                                 op0=ALU.mult, op1=ALU.add).then_inc(a_chain, 1)

            def ada_bias(b, i=0):
                dve.wait_ge(acc_red, b + 1 + i)
                at = bass.ds(i * 4 + 4 * b, 4)
                dve.tensor_tensor(MOD[:, at], ADP, VC[:, at], ALU.add).then_inc(mod_ready, 1)

            def wait_tile(stage, group, n, last_unit):
                if n < 2:
                    dve.wait_ge(bank_done, BD[stage] + group + 1)
                else:
                    dve.wait_ge(w_used, last_unit + 1)

            def add_tile(layer, chunk, j, mods):
                if j == 0:
                    dve.wait_ge(mod_ready, mods)
                dve.scalar_tensor_tensor(out=X[:, j, :], in0=M[:, j, :], scalar=mod(layer, chunk, j), in1=X[:, j, :],
                                         op0=ALU.mult, op1=ALU.add).then_inc(x_ready, 1)

            def norm(n):
                dve.wait_ge(mod_ready, MODS_BY_NORM[n])
                if n > 0:
                    dve.wait_ge(t_ready, KT * n)
                if n == 1:
                    dve.wait_ge(vc_ready, ROW_TILES)
                name, at = GAINS[n]
                dve.scalar_tensor_tensor(out=COEF[:, :], in0=mod(n // 2, 3 * (n % 2) + 1, 0, KT), scalar=1.0,
                                         in1=vc(name, at, KT), op0=ALU.add, op1=ALU.mult).then_inc(coef_ready, 1)
                dve.wait_ge(std_ready, n + 1)
                dve.reciprocal(RSTD[:, :], STD[:, :]).then_inc(rstd_ready, 1)
                dve.wait_ge(coef_ready, n + 1)
                dve.wait_ge(rstd_spread, n + 1)
                fill = 3 * (n // 2) + 2 * (n % 2)
                for j in range(KT + 2):
                    if j < KT:
                        dve.scalar_tensor_tensor(out=TMP[:, j, :], in0=X[:, j, :], scalar=COEF[:, j:j + 1], in1=AUX[:, 1, :],
                                                 op0=ALU.mult, op1=ALU.mult).then_inc(t_ready, 1)
                    if j >= 2 and n < 6:
                        q = j - 2
                        dve.wait_ge(hh_ready, KT * fill + q + 1)
                        dve.scalar_tensor_tensor(out=XL[:, q, :], in0=TMP[:, q, :], scalar=mod(n // 2, 3 * (n % 2), q),
                                                 in1=XH[:, q, :], op0=ALU.add, op1=ALU.subtract).then_inc(xin_ready, 1)

            def feed_forward(layer, before):
                base, m0 = U0[f"gu{layer}"], FT * layer
                b0, steps = GU_BLOCKS[layer]
                second = int(layer >= 1)

                def products(i, g):
                    for n in range(2):
                        m = i * 4 + (m0 + 2 * g + n)
                        dve.wait_ge(silu_ready, m + 1)
                        dve.wait_ge(w_used, i * 4 + U0[f"gu{layer}"] + 2 * g + 2)
                        dve.tensor_tensor(TMP[:, 4 + 2 * g + n, :], TMP[:, 2 * g + n, :], M[:, 4 * g + 2 + n, :],
                                          ALU.mult).then_inc(midf_ready, 1)

                def product_lows(i, g):
                    for n in range(2):
                        m = i * 4 + (2 * g + n)
                        dve.wait_ge(midh_ready, m + m0 + 1)
                        at = bass.ds(m * T, T)
                        dve.tensor_tensor(MLF[:, at], TMP[:, 4 + 2 * g + n, :], MHF[:, at], ALU.subtract).then_inc(mid_ready, 1)

                low(base, 0)
                low(base, 1)
                before()
                norm(2 * layer + 1)
                low(base, 2)
                low(base, 3)
                ada_sum(b0, second)
                with dve.Fori(1, 5) as i:
                    low(base, 0, i)
                    low(base, 1, i)
                    products(i - 1, 0)
                    ada_bias(b0, i - 1)
                    ada_sum(b0, second, i, rows=range(0, 4))
                    product_lows(i - 1, 0)
                    low(base, 2, i)
                    products(i - 1, 1)
                    low(base, 3, i)
                    product_lows(i - 1, 1)
                    ada_sum(b0, second, i, rows=range(4, 8))
                low(base, 20)
                low(base, 21)
                products(4, 0)
                ada_bias(b0 + 4)
                product_lows(4, 0)
                base = U0[f"dn{layer}"]
                low(base, 0)
                products(4, 1)
                low(base, 1)
                product_lows(4, 1)
                if 5 in steps:
                    ada_sum(b0 + 5, second)
                products(5, 0)
                product_lows(5, 0)
                if 5 in steps:
                    ada_bias(b0 + 5)
                b0 = DN_BLOCKS[layer]
                with dve.Fori(0, 2) as i:
                    low(base, 2, i)
                    low(base, 3, i)
                    if b0 is not None:
                        ada_sum(b0, layer, i)
                    low(base, 4, i)
                    low(base, 5, i)
                    if b0 is not None:
                        ada_bias(b0, i)
                low(base, 10)

            def add_down(layer):
                for j in range(KT):
                    if j < KT - 2:
                        dve.wait_ge(bank_done, BD[f"dn{layer}"] + j // 2 + 1)
                    else:
                        dve.wait_ge(w_used, U0[f"dn{layer}"] + 11)
                    add_tile(layer, 5, j, MODS_BY_DOWN[layer])

            def add_out(stage, layer, g):
                for n in range(4):
                    wait_tile(stage, g, n, U0[stage] + 2 * g + 1)
                    add_tile(layer, 2, 4 * g + n, MODS_BY_OUT[layer])

            dve.wait_ge(const_in, 16)
            dve.tensor_copy(IDB[:, :], IDENT).then_inc(masks_ready, 1)
            dve.wait_ge(pos_in, 16)
            A0, A1, A2, A3 = (ANG[:, q, :] for q in range(4))
            dve.tensor_copy(A3, POSI[:, :]).then_inc(ang_v, 1)
            dve.wait_ge(ang_v, 1)
            dve.tensor_scalar(A0, A3, cc(C_INVF), None, ALU.mult).then_inc(ang_v, 1)
            dve.wait_ge(ang_v, 2)
            dve.tensor_scalar(A1, A0, float(1 / (2 * np.pi)), ROUND, ALU.mult, ALU.add).then_inc(ang_v, 1)
            dve.wait_ge(ang_v, 3)
            dve.tensor_scalar(A2, A1, -ROUND, None, ALU.add).then_inc(ang_v, 1)
            for q, part in enumerate(two_pi_parts()):
                dve.wait_ge(ang_v, 4 + q)
                src, dst = (A0, A1) if q % 2 == 0 else (A1, A0)
                dve.scalar_tensor_tensor(out=dst, in0=A2, scalar=-part, in1=src, op0=ALU.mult, op1=ALU.add).then_inc(ang_v, 1)
            dve.wait_ge(ang_v, 8)
            dve.tensor_scalar(A0, A0, 3.1415925, -3.1415925, ALU.min, ALU.max).then_inc(ang_v, 1)
            dve.wait_ge(ang_v, 9)
            dve.scalar_tensor_tensor(out=A1, in0=A0, scalar=-1.0, in1=A0, op0=ALU.mult, op1=ALU.min).then_inc(ang_v, 1)

            dve.wait_ge(cond_ready, 1)
            ada_sum(0, 0)
            for b in range(1, 4):
                ada_sum(b, 0)
                if b == 1:
                    dve.wait_ge(vc_ready, len(EARLY_ROWS))
                ada_bias(b - 1)
            low(U0["qkv_a"], 0)
            ada_bias(3)
            dve.wait_ge(ang_s, 2)
            dve.tensor_scalar(COS[:, :], COS[:, :], cc(C_ROPE), cc(C_KEEP), ALU.mult, ALU.add).then_inc(trig_ready, 1)
            dve.tensor_scalar(vc("q_norm_a", 0), vc("q_norm_a", 0), SCALE, None, ALU.mult).then_inc(gain_ready, 1)
            norm(0)
            base = U0["qkv_a"]
            for k in range(1, 4):
                low(base, k)

            def qa_recip(g):
                n = len(QA_GROUPS[g])
                dve.wait_ge(qa_std, g + 1)
                dve.reciprocal(QRS[:, g, 0:4 * n], QSTD[:, g, 0:4 * n]).then_inc(qa_rs, 1)

            def qa_keys():
                dve.wait_ge(qa_spread, 1)
                dve.tensor_tensor(QN[:, 0, :], QA[:, 8, :], M[:, 2, :], ALU.mult).then_inc(qa_n, 1)

            def qa_rope(i):
                if i == 0:
                    dve.wait_ge(qa_n, 1)
                else:
                    dve.wait_ge(qa_gain, i + 1)
                dve.tensor_tensor(QA[:, QA_ROWS[i], :], QN[:, i % 4, :], COS[:, :], ALU.mult).then_inc(qa_c, 1)
                dve.wait_ge(qa_rot, i + 1)
                if i >= 2:
                    dve.wait_ge(qa_q, i - 1)
                dve.tensor_tensor(QT2[:, i % 2, :], AUX[:, 4, :], SIN[:, :], ALU.mult).then_inc(qa_t2, 1)

            def qa_add(i):
                dve.wait_ge(qa_t2, i + 1)
                dve.tensor_tensor(QA[:, QA_ROWS[i], :], QA[:, QA_ROWS[i], :], QT2[:, i % 2, :], ALU.add).then_inc(qa_q, 1)

            def qa_group(g):
                for i in QA_GROUPS[g]:
                    qa_rope(i)
                    qa_add(i)

            dve.wait_ge(misc_in, 48)
            dve.tensor_copy(MASKA[:, :], CTMP[:, T0["mask_a"]:T0["mask_a"] + 3 * P]).then_inc(masks_ready, 1)
            dve.tensor_copy(MASKB[:, :], CTMP[:, T0["mask_b"]:T0["mask_b"] + P]).then_inc(masks_ready, 1)
            dve.tensor_scalar(NSINK[:, :, :], SINK[:, :, :], -1.0, None, ALU.mult).then_inc(sink_ready, 1)
            dve.wait_ge(trig_ready, 1)
            ada_sum(4, 0, rows=range(0, 4))
            qa_recip(0)
            qa_keys()
            qa_group(0)
            ada_sum(4, 0, rows=range(4, 8))
            low(base, 4)
            ada_bias(4)
            ada_sum(5, 0)
            qa_group(1)
            low(U0["wo_a"], 0)
            ada_bias(5)

            def query_roots(b):
                at = 4 * (b % 4)
                return QRS[:, 1 + b // 4, at:at + 4].rearrange("p (k e) -> p e k", e=2)

            def sa_max(b):
                p = b % 2
                if b >= 2:
                    dve.wait_ge(sa_r, b - 1)
                dve.wait_ge(sa_s, b + 1)
                for blk, lo, hi in ((0, 0, P), (1, P, 3 * P)):
                    dve.reduce_max(SM[:, p, 0, blk:4:2], MB[:, 2 - 2 * p:4 - 2 * p, lo:hi], AX_X).then_inc(sa_m, 1)
                dve.wait_ge(sa_m, 2 * b + 2)
                if b == 0:
                    dve.wait_ge(sink_ready, 1)
                if b >= 2:
                    dve.wait_ge(sa_e, b - 1)
                nsink = NSINK[:, :, 2 * b:2 * b + 2].rearrange("p k e -> p e k")
                sink = SINK[:, :, 2 * b:2 * b + 2].rearrange("p k e -> p e k")

                def small(row):
                    return SM[:, p, row, :].rearrange("p (e k) -> p e k", k=2)

                if b in (0, 4):
                    dve.wait_ge(qa_rs, 2 + b // 4)
                dve.tensor_tensor(small(0), small(0), query_roots(b), ALU.mult).then_inc(sa_mr, 1)
                dve.wait_ge(sa_mr, b + 1)
                dve.scalar_tensor_tensor(out=small(1), in0=small(0), scalar=-1.0, in1=nsink,
                                         op0=ALU.mult, op1=ALU.min).then_inc(sa_nm, 1)
                dve.wait_ge(sa_nm, b + 1)
                dve.tensor_tensor(small(2), sink, small(1), ALU.add).then_inc(sa_d, 1)

            def sa_divide(b):
                p = b % 2
                dve.wait_ge(sa_p, 4 * b + 4)
                dve.wait_ge(sa_e, b + 1)
                if b >= 2:
                    dve.wait_ge(sa_pn, 4 * b - 4)
                dve.tensor_tensor(SM[:, p, 4, :], RS_SUM[:, p, :], SM[:, p, 3, :], ALU.add).then_inc(sa_t, 1)
                dve.wait_ge(sa_t, b + 1)
                dve.reciprocal(SM[:, p, 5, :], SM[:, p, 4, :]).then_inc(sa_r, 1)

            def attn_low(fill, b):
                dve.wait_ge(hh_ready, KT * fill + b + 1)
                o = AUX[:, 4, :] if fill == 1 else AUX[:, 4 - 4 * (b % 2), :]
                dve.tensor_tensor(XL[:, b, :], o, XH[:, b, :], ALU.subtract).then_inc(xin_ready, 1)

            qa_recip(1)
            sa_max(0)
            qa_group(2)
            sa_divide(0)
            sa_max(1)
            for b in range(8):
                if b + 1 < 8:
                    sa_divide(b + 1)
                if b == 1:
                    qa_recip(2)
                if b + 2 < 8:
                    sa_max(b + 2)
                if b % 2 == 0 and b > 0:
                    ada_bias(5 + b // 2)
                half = KT // 2 * (b % 2)
                ada_sum(6 + b // 2, 0, rows=range(half, half + KT // 2))
                attn_low(1, b)
                if b in (1, 3, 5):
                    low(U0["wo_a"], (b + 1) // 2)
            ada_bias(9)
            ada_sum(10, 0)
            add_out("wo_a", 0, 0)

            def before_ffn_a():
                ada_bias(10)
                add_out("wo_a", 0, 1)
            feed_forward(0, before_ffn_a)

            base = U0["qkv_b"]
            low(base, 0)
            low(base, 1)
            add_down(0)
            norm(2)
            low(base, 2)
            low(base, 3)
            ada_sum(19, 0)
            for k in range(4, 8):
                low(base, k)
            ada_bias(19)
            for q in range(2):
                ada_sum(20 + q, 0)
                low(base, 8 + 2 * q)
                low(base, 9 + 2 * q)
                ada_bias(20 + q)
            ada_sum(22, 0)
            for k in range(2):
                low(U0["wo_b"], k)
            ada_bias(22)
            for k in range(2, 4):
                low(U0["wo_b"], k)

            def sb_abs(h):
                z = MB[:, h % 4, 0:384]
                dve.wait_ge(sb_z, h + 1)
                if h >= 3:
                    dve.wait_ge(sb_sp, h - 2)
                dve.tensor_scalar(ZP[:, h % 3, :], z, 0.0, None, ALU.max).then_inc(sb_zp, 1)
                dve.wait_ge(sb_zp, h + 1)
                dve.scalar_tensor_tensor(out=AZ[:, h % 3, :], in0=ZP[:, h % 3, :], scalar=-2.0, in1=z,
                                         op0=ALU.mult, op1=ALU.add).then_inc(sb_az, 1)

            def sb_plus(h):
                dve.wait_ge(sb_ln, h + 1)
                if h >= 3:
                    dve.wait_ge(sb_e, h - 2)
                dve.tensor_tensor(SP[:, h % 3, :], ZP[:, h % 3, :], AZ[:, h % 3, :], ALU.add).then_inc(sb_sp, 1)

            sb_abs(0)
            sb_abs(1)
            for h in range(16):
                sb_plus(h)
                if h >= 3 and h % 2 == 1:
                    attn_low(4, (h - 3) // 2)
                if h + 2 < 16:
                    sb_abs(h + 2)
                if h < 4 * len(STICK_BLOCKS):
                    b, r = STICK_BLOCKS[h // 4], 2 * (h % 4)
                    if r == 2 and h > 4:
                        ada_bias(b - 1)
                    ada_sum(b, int(b >= 24), rows=range(r, r + 2))
                elif h == 4 * len(STICK_BLOCKS) + 1:
                    ada_bias(STICK_BLOCKS[-1])
            attn_low(4, 7)
            add_out("wo_b", 1, 0)
            feed_forward(1, lambda: add_out("wo_b", 1, 1))

            base = U0["w_in"]
            low(base, 0)
            low(base, 1)
            add_down(1)
            norm(4)
            low(base, 2)
            low(base, 3)
            dve.wait_ge(mx_in, 112)
            dve.tensor_tensor(WSP[:, :, :], WSP[:, :, :], TRIL[:, :].unsqueeze(1).to_broadcast([P, 8, P]), ALU.mult).then_inc(mx_tril, 1)
            dve.memset(Y0[:, :, 0:CONV - 1], 0.0).then_inc(mx_pad, 1)
            low(base, 4)
            low(base, 5)
            for j in range(4):
                dve.wait_ge(mx_sg, j + 1)
                wait_tile("w_in", 1, j, base + 3)
                dve.scalar_tensor_tensor(out=Y0[:, j, CONV - 1:], in0=M[:, 4 + j, :], scalar=vc("b_in_2", 8 + j), in1=SG[:, j, :],
                                         op0=ALU.add, op1=ALU.mult).then_inc(mx_y0, 1)
            low(base, 6)
            low(base, 7)

            def tap(k, j):
                at = bass.ds(k, T) if not isinstance(k, int) else slice(k, k + T)
                w = COL["b_conv_w_2"] + j
                return Y0[:, j, at], VC[:, bass.ds(k * 4 + w, 1)]

            def taps(lo, hi):
                with dve.Fori(lo, hi) as k:
                    for j in range(4):
                        src, w = tap(k, j)
                        dve.wait_ge(cv_c, k * 4 + (j - 3 - 4 * PE_TAPS))
                        dve.scalar_tensor_tensor(out=CV[:, j, :], in0=src, scalar=w, in1=CV[:, j, :],
                                                 op0=ALU.mult, op1=ALU.add).then_inc(cv_c, 1)

            dve.wait_ge(mx_pad, 1)
            dve.wait_ge(mx_y0, 4)
            for j in range(4):
                src, w = tap(PE_TAPS, j)
                dve.tensor_scalar(CV[:, j, :], src, w, vc("b_conv_b_2", j), ALU.mult, ALU.add).then_inc(cv_c, 1)
            taps(PE_TAPS + 1, CONV)
            ada_sum(MIX_BLOCK, 1)
            for j in range(4):
                dve.wait_ge(dg_used, 4 * PE_TAPS - 2 + 2 * (j // 2))
                dve.wait_ge(cv_c, 4 * (CONV - PE_TAPS))
                dve.tensor_tensor(CV[:, j, :], CV[:, j, :], AUX[:, j, :], ALU.add).then_inc(cv_ready, 1)
            for j in range(4):
                dve.wait_ge(gn_mu, j // 2 + 1)
                dve.tensor_tensor(CV[:, j, :], CV[:, j, :], AUX[:, j, :], ALU.subtract).then_inc(gn_c, 1)
            low(U0["w_out"], 0)
            ada_bias(MIX_BLOCK)
            for m in range(2):
                if m == 0:
                    dve.wait_ge(bank_done, BD["w_in"] + 3)
                else:
                    dve.wait_ge(w_used, base + 6)
                dve.tensor_tensor(VX[:, m, :], MB[:, m, :], BV[:, :], ALU.add).then_inc(v_x, 1)
            dve.wait_ge(gn_std, 1)
            dve.reciprocal(GRS[:, :], GSTD[:, :]).then_inc(gn_rs, 1)
            for m in range(2):
                dve.wait_ge(v_g, m + 1)
                dve.tensor_scalar(VST[:, m, 1:2], VST[:, m, 0:1], 1.0 / DA, None, ALU.mult).then_inc(v_mu, 1)
            for m in range(2):
                dve.wait_ge(v_mu, m + 1)
                dve.tensor_scalar(VX[:, m, :], VN[:, m, :], VST[:, m, 1:2], None, ALU.subtract).then_inc(v_c, 1)
            for j in range(4):
                dve.wait_ge(gn_spread, j // 2 + 1)
                dve.tensor_tensor(CV[:, j, :], CV[:, j, :], AUX[:, j, :], ALU.mult).then_inc(gn_n, 1)
            for m in range(2):
                dve.wait_ge(v_sd, m + 1)
                dve.reciprocal(VST[:, m, 4:5], VST[:, m, 3:4]).then_inc(v_rs, 1)
            for m in range(2):
                dve.wait_ge(v_rs, m + 1)
                dve.scalar_tensor_tensor(out=VN[:, m, :], in0=VX[:, m, :], scalar=VST[:, m, 4:5], in1=LNG[:, :],
                                         op0=ALU.mult, op1=ALU.mult).then_inc(v_n, 1)
            for m in range(2):
                dve.wait_ge(v_n, m + 1)
                dve.tensor_tensor(VN[:, m, :], VN[:, m, :], LNB[:, :], ALU.add).then_inc(v_b, 1)
            low(U0["w_out"], 1)

            def out_norm(turn, rows, name):
                q = 1 - turn
                dve.wait_ge(on_std, turn + 1)
                dve.reciprocal(RSTD[:, :], STD[:, :]).then_inc(on_rs, 1)
                dve.wait_ge(on_spread, turn + 1)
                for j in range(4):
                    dve.scalar_tensor_tensor(out=TMP[:, 4 * q + j, :], in0=rows[:, j, :], scalar=vc(name, j), in1=ON_SPREAD[turn],
                                             op0=ALU.mult, op1=ALU.mult).then_inc(on_t, 1)
                for j in range(4):
                    dve.wait_ge(hh_ready, KT * 7 + 4 * turn + j + 1)
                    dve.tensor_tensor(XL[:, 4 * q + j, :], TMP[:, 4 * q + j, :], XH[:, 4 * q + j, :], ALU.subtract).then_inc(xin_ready, 1)

            out_norm(0, SG, "out_norm_b_g_2")
            low(U0["w_out"], 2)
            for j in range(4):
                dve.wait_ge(sp_done, j // 2 + 1)
                bias = BSB[:, j, :].unsqueeze(1).to_broadcast([P, 2, P])
                dve.tensor_tensor(TMP[:, j, :].rearrange("p (c t) -> p c t", c=2), AUX[:, j, :].rearrange("p (c t) -> p c t", c=2),
                                  bias, ALU.add).then_inc(ya_t, 1)
            for j in range(4):
                dve.wait_ge(ya_t, j + 1)
                dve.wait_ge(ug_ready, j + 1)
                dve.tensor_tensor(UG[:, j, :], TMP[:, j, :], UG[:, j, :], ALU.mult).then_inc(ya_ready, 1)
            low(U0["w_out"], 3)
            out_norm(1, UG, "out_norm_a_g_2")
            for n in range(4):
                if n < 2:
                    dve.wait_ge(bank_done, BD["w_out"] + 1)
                else:
                    dve.wait_ge(w_used, U0["w_out"] + 3)
                add_tile(2, 2, n, MODS_BY_OUT[2])
            feed_forward(2, lambda: add_out("w_out", 2, 1))
            add_down(2)
            norm(6)

        @block.tensor
        def _(pe):
            def three(out_ap, wh, wl, xh, xl, start, stop):
                pe.matmul(out_ap, wh, xh, start=start, stop=False, skip_group_check=True)
                pe.matmul(out_ap, wh, xl, start=False, stop=False, skip_group_check=True)
                return pe.matmul(out_ap, wl, xh, start=False, stop=stop, skip_group_check=True)

            def unit(base, k, i, taus, kts, x_of, first, last, by_rows=None, between=None):
                s = slot(base, k)
                pe.wait_ge(l_ready, base + k + 1 + 4 * i)
                width = 2048 // len(kts)
                pairs = [(q, n) for n in range(len(taus)) for q in range(len(kts))]
                if by_rows is not None:
                    pairs = [(q, n) for q in range(len(kts)) for n in range(len(taus))]
                for at, (q, n) in enumerate(pairs):
                    if by_rows is not None and n == 0:
                        pe.wait_ge(xin_ready, KT * by_rows + kts[q] + 1)
                    tau, col = taus[n]
                    xh, xl = x_of(kts[q])
                    cols = slice(q * width + col, q * width + col + P)
                    ends = last and q == len(kts) - 1
                    mm = three(M[:, tau, :], WH[:, s, cols], WL[:, s, cols], xh, xl,
                               first and q == 0 and tau % 2 == 0, ends)
                    if at == len(pairs) - 1:
                        mm.then_inc(w_used, 1)
                    elif ends and tau % 2 == 1:
                        mm.then_inc(bank_done, 1)
                    if between is not None and q == len(kts) - 1 and n < len(taus) - 1:
                        between[n]()

            def operand(kt):
                return XH[:, kt, :], XL[:, kt, :]

            def group(base, g, st, i=0, fill=None, middle=None, between=None):
                taus = [(4 * st + n, n * P) for n in range(4)]
                unit(base, 2 * g, i, taus, range(0, 4), operand, True, False, fill)
                if fill is not None:
                    pe.wait_ge(xin_ready, KT * fill + KT)
                if middle is not None:
                    middle()
                unit(base, 2 * g + 1, i, taus, range(4, 8), operand, False, True, between=between)

            def early_means(n):
                return [lambda: mean_square(n, 0), lambda: [mean_square(n, 1), mean_square(n, 2)], lambda: mean_square(n, 3)]

            def values(base, k, kts, col, width, outs, first, last):
                s = slot(base, k)
                pe.wait_ge(l_ready, base + k + 1)
                row = 2048 // len(kts)
                for m in range(2):
                    for q, kt in enumerate(kts):
                        rows = slice(m * P, m * P + P)
                        wh, wl = (w[:, s, q * row + col:q * row + col + width] for w in (WH, WL))
                        start = first and q == 0 and outs[m][1]
                        ends = last and q == len(kts) - 1
                        pe.matmul(outs[m][0], XH[:, kt, rows], wh, start=start, stop=False, skip_group_check=True)
                        pe.matmul(outs[m][0], XL[:, kt, rows], wh, start=False, stop=False, skip_group_check=True)
                        mm = pe.matmul(outs[m][0], XH[:, kt, rows], wl, start=False, stop=ends, skip_group_check=True)
                    if m == 1:
                        mm.then_inc(w_used, 1)
                    elif last and width == 512:
                        mm.then_inc(bank_done, 1)

            def ada_reduce(b, i=0):
                pe.wait_ge(a_chain, 8 * b + 8 + 8 * i)
                if b > 0:
                    pe.wait_ge(mod_ready, b + i)
                for j in range(4):
                    mm = pe.matmul(AUX[:, 6, j:j + 1], ACC[:, acc_slot(b), j * P:(j + 1) * P], cc(C_ONE), start=True, stop=True)
                mm.then_inc(acc_red, 1)

            def mean_square(n, j):
                pe.wait_ge(sq_ready, KT * n + j + 1)
                mm = token_means(AUX[:, 0, 0:2], TMP[:, j, :], ONES[:, 0:1], j == 0, j == KT - 1)
                if j == KT - 1:
                    mm.then_inc(ssq_ready, 1)

            def norm(n, done=0, blocks=()):
                for j in range(done, KT):
                    mean_square(n, j)
                for b in blocks:
                    ada_reduce(b)
                pe.wait_ge(rstd_ready, n + 1)
                spread(AUX[:, 1, :], RSTD, 0).then_inc(rstd_spread, 1)

            def token_means(sums, squares, columns, first, last):
                n = columns.shape[1]
                for m in range(2):
                    mm = pe.matmul(sums[:, n * m:n * m + n], squares[:, m * P:(m + 1) * P], columns,
                                   start=first and m == 0, stop=last, skip_group_check=True)
                return mm

            def spread(out_ap, columns, at, step=1):
                for m in range(2):
                    col = columns[:, at + step * m:at + step * m + 1]
                    mm = pe.matmul(out_ap[:, m * P:(m + 1) * P], col.to_broadcast([P, out_ap.shape[0]]), IDENT,
                                   start=True, stop=True, skip_group_check=True)
                return mm

            def feed_forward(layer):
                base, m0 = U0[f"gu{layer}"], FT * layer
                b0, steps = GU_BLOCKS[layer]
                norm(2 * layer + 1, 4)
                group(base, 0, 0, 0, 3 * layer + 2)
                group(base, 1, 1)
                ada_reduce(b0)
                with pe.Fori(1, 5) as i:
                    for g in range(2):
                        pe.wait_ge(midf_ready, i * 4 + m0 + 2 * g - 2)
                        group(base, g, g, i, middle=(lambda: ada_reduce(b0, i)) if g == 1 else None)
                pe.wait_ge(midf_ready, m0 + 18)
                group(base, 10, 0)
                base = U0[f"dn{layer}"]

                def hidden(kt):
                    return MH[:, kt, :], ML[:, kt, :]

                def hidden_at(i, k):
                    def rows(kt):
                        at = bass.ds((i * 8 + kt) * T, T)
                        return MHF[:, at], MLF[:, at]
                    return rows

                pe.wait_ge(midf_ready, m0 + 20)
                pe.wait_ge(mid_ready, m0 + 18)
                down_unit(base, 0, hidden, [4, 5, 6, 7, 0, 1, 2, 3], m0 + 22, True, False)
                down_unit(base, 1, hidden, range(8), None, False, False)
                if 5 in steps:
                    ada_reduce(b0 + 5)
                pe.wait_ge(mid_ready, m0 + 22)
                b0 = DN_BLOCKS[layer]
                with pe.Fori(0, 2) as i:
                    for k in range(2, 6):
                        down_unit(base, k, hidden_at(i, k), range(8), None, False, False, i)
                        if k == 3 and b0 is not None:
                            ada_reduce(b0, i)
                n = 2 * layer + 2
                down_unit(base, 10, hidden, range(8), None, False, True,
                          between={4: [0], 5: [1], 6: [2, 3]}, norm_at=n)

            def down_unit(base, k, x_of, order, set0_free, first, ending, i=0, between=None, norm_at=None):
                s = slot(base, k)
                pe.wait_ge(l_ready, base + k + 1 + 4 * i)
                for at, n in enumerate(order):
                    if set0_free is not None and n == 0:
                        pe.wait_ge(midf_ready, set0_free)
                    for q in range(2):
                        xh, xl = x_of(2 * k + q)
                        cols = slice(q * D + n * P, q * D + n * P + P)
                        mm = three(M[:, n, :], WH[:, s, cols], WL[:, s, cols], xh, xl, first and q == 0 and n % 2 == 0, False)
                    if at == KT - 1:
                        mm.then_inc(w_used, 1)
                    elif ending and n % 2 == 1:
                        mm.then_inc(bank_done, 1)
                    for j in (between or {}).get(n, []):
                        mean_square(norm_at, j)

            pe.wait_ge(const_in, 16)
            pe.wait_ge(crows_in, 32)
            pe.transpose(AUX[:, 0, 0:2 * KT], CROWS[:, :], IDENT[0:2 * KT, 0:2 * KT]).then_inc(c_turned, 1)

            def turn_rows(tiles):
                for r in tiles:
                    n = ROWS_IN_TILE[r]
                    mm = pe.transpose(AUX[:, 2 + r // 2, (r % 2) * P:(r % 2) * P + n], VROWS[0:n, r, :], IDENT[0:n, 0:n])
                mm.then_inc(rows_turned, 1)

            pe.wait_ge(early_rows_in, 16 * row_dmas(EARLY_ROWS))
            turn_rows(EARLY_ROWS)
            pe.wait_ge(x_in, 16)
            for j in range(KT):
                for m in range(2):
                    mm = pe.transpose(M[:, j, m * P:(m + 1) * P], XTOK[:, m, j * P:(j + 1) * P], IDENT)
                if j % 2 == 1:
                    mm.then_inc(x_turned, 1)
            ada_reduce(0)
            norm(0, blocks=range(1, 4))

            base = U0["qkv_a"]

            def qa_mean(i):
                g, first = [(g, t[0]) for g, t in enumerate(QA_GROUPS) if i in t][0]
                pe.wait_ge(qa_sq, i + 1)
                if i == first and g == 1:
                    pe.wait_ge(vc_ready, ROW_TILES)
                if i == first and g == 2:
                    pe.wait_ge(qa_std, 1)
                at = 4 * (i - first)
                token_means(AUX[:, 2 * (g % 2), at:at + 4], QSQ[:, i % 2, :], BLK[:, 0:P:HD], i == first, True).then_inc(qa_ssq, 1)

            def spread_key_roots():
                pe.wait_ge(qa_rs, 1)
                for e in range(2):
                    mm = spread(M[HD * e:HD * e + HD, 2, :], QRS[:, 0, :], e, 2)
                mm.then_inc(qa_spread, 1)

            def qa_turn(i):
                if i == 0:
                    pe.wait_ge(qa_n, 1)
                else:
                    pe.wait_ge(qa_gain, i + 1)
                    pe.wait_ge(qa_t2, i)
                if i == 1:
                    pe.wait_ge(ks_ready, 1)
                pe.matmul(AUX[:, 4, :], ROTM, QN[:, i % 4, :], start=True, stop=True).then_inc(qa_rot, 1)

            def swap_keys():
                pe.wait_ge(qa_q, 1)
                pe.matmul(AUX[:, 4, :], CTMP[:, T0["swap"]:T0["swap"] + P], QA[:, 8, :], start=True, stop=True).then_inc(ks_t, 1)

            pe.wait_ge(l_ready, base + 1)
            for kt in range(KT):
                pe.wait_ge(xin_ready, kt + 1)
                cols = slice(kt * 256, kt * 256 + P)
                three(M[:, 0, :], WH[:, 0, cols], WL[:, 0, cols], *operand(kt), kt == 0, kt == KT - 1)
                cols = slice(kt * 256 + P, kt * 256 + 2 * P)
                mm = three(M[:, 1, :], WH[:, 0, cols], WL[:, 0, cols], *operand(kt), False, kt == KT - 1)
            mm.then_inc(w_used, 1)
            pe.wait_ge(misc_in, 48)
            sets = [[(4 + n, n * P) for n in range(4)], [(n, n * P) for n in range(4)]]
            unit(base, 1, 0, sets[0], range(0, 4), operand, True, False)
            qa_mean(0)
            pe.wait_ge(late_rows_in, 16 * row_dmas(LATE_ROWS))
            pe.wait_ge(v_turn, 1)
            for m in range(2):
                mm = pe.transpose(M[:, 1, m * P:(m + 1) * P], VTURN[:, m * P:(m + 1) * P], IDENT)
            mm.then_inc(v_turned, 1)
            pe.wait_ge(vc_ready, len(EARLY_ROWS))
            turn_rows(LATE_ROWS)
            unit(base, 2, 0, sets[0], range(4, 8), operand, False, True,
                 between=[spread_key_roots, lambda: qa_turn(0), lambda: None])
            ada_reduce(4)
            pe.wait_ge(qa_gain, 1)
            pe.wait_ge(va_ready, 1)
            swap_keys()
            unit(base, 3, 0, sets[1], range(0, 4), operand, True, False,
                 between=[lambda: None, lambda: [qa_mean(i) for i in range(1, 5)], lambda: qa_turn(1)])
            ada_reduce(5)
            unit(base, 4, 0, sets[1], range(4, 8), operand, False, True,
                 between=[lambda: qa_turn(2), lambda: qa_turn(3), lambda: qa_turn(4)])

            def sa_scores(b):
                for e in range(2):
                    rows = slice(HD * e, HD * e + HD)
                    keys = QA[rows, 8, :] if e == b // 4 else KS[rows, :]
                    bank = MB[:, 2 - 2 * (b % 2) + e, :]
                    pe.matmul(bank[:, 0:P], QA[rows, b, 0:P], keys[:, 0:P], start=True, stop=False, skip_group_check=True)
                    pe.matmul(bank[:, P:3 * P], QA[rows, b, P:2 * P], keys, start=False, stop=False, skip_group_check=True)
                    mm = pe.matmul(bank[:, 0:3 * P], IDB[:, :], MASKA[:, :], start=False, stop=True, skip_group_check=True)
                mm.then_inc(sa_s, 1)

            def sa_turn(b):
                for e in range(2):
                    pe.wait_ge(sa_pn, 4 * b + 2 * e + 2)
                    if b >= 1:
                        pe.wait_ge(sa_ptc, 2 * (b - 1) + e + 1)
                    for blk in range(3):
                        cols = slice(blk * P, blk * P + P)
                        mm = pe.transpose(AB4[:, e, cols], PR[:, b % 2, e, cols], IDENT)
                    mm.then_inc(sa_tr, 1)

            def sa_rows(b):
                kv = slice(HD * (b // 4), HD * (b // 4) + HD)
                if b >= 1:
                    pe.wait_ge(xin_ready, KT + b)
                for e in range(2):
                    pe.wait_ge(sa_ptc, 2 * b + e + 1)
                    rows = slice(HD * e, HD * e + HD)
                    o = AUX[rows, 4, :]
                    pe.matmul(o[:, 0:P], VA[:, 0, kv], PT[:, b % 2, e, 0:P], start=True, stop=True, skip_group_check=True)
                    pe.matmul(o[:, P:2 * P], VA[:, 0, kv], PT[:, b % 2, e, P:2 * P], start=True, stop=False, skip_group_check=True)
                    mm = pe.matmul(o[:, P:2 * P], VA[:, 1, kv], PT[:, b % 2, e, 2 * P:3 * P], start=False, stop=True, skip_group_check=True)
                mm.then_inc(sa_o, 1)

            pe.wait_ge(masks_ready, 3)
            pe.wait_ge(qa_q, 5)
            sa_scores(0)
            for i in range(5, 9):
                qa_mean(i)
                qa_turn(i)
            pe.wait_ge(qa_q, 9)
            sa_scores(1)
            for b in range(8):
                sa_turn(b)
                if b + 2 < 8:
                    sa_scores(b + 2)
                if b % 2 == 0 and b > 0:
                    ada_reduce(5 + b // 2)
                sa_rows(b)
            ada_reduce(9)
            group(U0["wo_a"], 0, 0, 0, 1)
            group(U0["wo_a"], 1, 1, middle=lambda: ada_reduce(10), between=early_means(1))
            feed_forward(0)

            base = U0["qkv_b"]
            norm(2, 4)
            group(base, 0, 0, 0, 3)
            group(base, 1, 1)
            ada_reduce(19)
            for g in range(2, 4):
                pe.wait_ge(qb_ev, 4 * g - 4)
                group(base, g, g % 2)
                ada_reduce(18 + g)
            for g in range(4, 6):
                pe.wait_ge(qb_ev, 4 * g - 4)
                outs = [(MB[:, 2 * (g % 2) + m, :], True) for m in range(2)]
                for k in range(2):
                    values(base, 2 * g + k, range(4 * k, 4 * k + 4), 0, 512, outs, k == 0, k == 1)
                if g == 4:
                    ada_reduce(22)

            def sb_scores(h):
                t, rows = h // 2, slice(HD * (h % 2), HD * (h % 2) + HD)
                if h >= 4:
                    pe.wait_ge(sb_a, h - 3)
                bank = MB[:, h % 4, :]
                pe.matmul(bank[:, 0:2 * P], KB[rows, t, 0:P], QB[rows, t, :], start=True, stop=False, skip_group_check=True)
                pe.matmul(bank[:, 2 * P:3 * P], KB[rows, t, P:2 * P], QB[rows, t, P:2 * P], start=False, stop=False, skip_group_check=True)
                pe.matmul(bank[:, 0:P], IDB[:, :], MASKB[:, :], start=False, stop=False, skip_group_check=True)
                pe.matmul(bank[:, 2 * P:3 * P], IDB[:, :], MASKB[:, :], start=False, stop=True, skip_group_check=True).then_inc(sb_z, 1)

            def sb_logs(h):
                pe.wait_ge(sb_sp, h + 1)
                bank, sp_ = MB[:, h % 4, :], SP[:, h % 3, :]
                pe.matmul(bank[:, 0:2 * P], TNEG, sp_[:, 0:2 * P], start=False, stop=False, skip_group_check=True)
                pe.matmul(bank[:, P:2 * P], ONEG, sp_[:, 2 * P:3 * P], start=False, stop=False, skip_group_check=True)
                pe.matmul(bank[:, 2 * P:3 * P], TNEG, sp_[:, 2 * P:3 * P], start=False, stop=True, skip_group_check=True).then_inc(sb_e, 1)

            def sb_rows(h):
                t, e = h // 2, h % 2
                if t >= 2:
                    pe.wait_ge(xin_ready, KT * 4 + t - 1)
                pe.wait_ge(sb_a, h + 1)
                o = AUX[HD * e:HD * e + HD, 4 - 4 * (t % 2), :]
                v = slice(HD * h, HD * h + HD)
                pe.matmul(o, VB[:, 0, v], AB[:, h % 2, 0:2 * P], start=True, stop=False, skip_group_check=True)
                pe.matmul(o[:, P:2 * P], VB[:, 1, v], AB[:, h % 2, 2 * P:3 * P], start=False, stop=True, skip_group_check=True).then_inc(sb_o, 1)

            pe.wait_ge(qb_ev, 20)
            sb_scores(0)
            sb_scores(1)
            for h in range(16 + 1):
                if h + 2 < 16:
                    sb_scores(h + 2)
                if h < 16:
                    sb_logs(h)
                if h >= 1:
                    sb_rows(h - 1)
                if h % 4 == 3 and h < 4 * len(STICK_BLOCKS):
                    ada_reduce(STICK_BLOCKS[h // 4])
            group(U0["wo_b"], 0, 0, 0, 4)
            group(U0["wo_b"], 1, 1, between=early_means(3))
            feed_forward(1)

            base = U0["w_in"]
            norm(4, 4)
            group(base, 0, 0, 0, 6)
            pe.wait_ge(mx_tril, 1)
            for h in range(8):
                mm = pe.transpose(AB4[:, h // 4, (h % 4) * P:(h % 4) * P + P], WSP[:, h, :], IDENT)
            mm.then_inc(mx_wt_t, 1)
            group(base, 1, 1)
            pe.wait_ge(mx_wt, 2)
            pe.wait_ge(mx_pad, 1)
            pe.wait_ge(mx_y0, 4)

            def two_taps(i, k0, first, last):
                for q in range(DIAGS):
                    j, k = q % 4, q // 4
                    pe.wait_ge(dg_ready, i * DIAGS + (4 * k0 + q + 1))
                    rows = Y0[:, j, bass.ds(i * 2 + (k0 + k), T)] if not isinstance(i, int) else Y0[:, j, k0 + k:k0 + k + T]
                    pe.matmul(AUX[:, j, :], WSP[:, q, :], rows, start=first and k == 0 and j % 2 == 0, stop=last and k == 1,
                              skip_group_check=True).then_inc(dg_used, 1)

            two_taps(0, 0, True, False)
            with pe.Fori(1, PE_TAPS // 2 - 1) as i:
                two_taps(i, 0, False, False)
            two_taps(0, PE_TAPS - 2, False, True)
            pe.wait_ge(mx_sg, 4)
            outs = [(MB[:, m, :], True) for m in range(2)]
            values(base, 4, range(0, 4), 0, 512, outs, True, False)
            for j in range(4):
                pe.wait_ge(cv_ready, 2 + 2 * (j // 2))
                mm = pe.matmul(AUX[:, j, :], BLK, CV[:, j, :], start=True, stop=True, skip_group_check=True)
                if j % 2 == 1:
                    mm.then_inc(gn_mu, 1)
            ada_reduce(MIX_BLOCK)
            values(base, 5, range(4, 8), 0, 512, outs, False, True)
            for j in range(4):
                pe.wait_ge(gn_sq, j + 1)
                mm = token_means(AUX[:, 5, 4 * j:4 * j + 4], TMP[:, 4 + j, :], BLK[:, 0:P:HD], j == 0, True)
            mm.then_inc(gn_var, 1)
            taus = [(4 + n, n * P) for n in range(4)]
            unit(base, 6, 0, taus, range(0, 4), operand, True, False)
            pe.wait_ge(gn_rs, 1)
            pe.wait_ge(gn_c, 4)
            for j in range(4):
                for e in range(2):
                    mm = spread(AUX[HD * e:HD * e + HD, j, :], GRS, 4 * j + e, 2)
                if j % 2 == 1:
                    mm.then_inc(gn_spread, 1)
            unit(base, 7, 0, taus, range(4, 8), operand, False, True)

            def out_norm(turn):
                for j in range(4):
                    pe.wait_ge(on_sq, 4 * turn + j + 1)
                    mm = token_means(ON_SUMS[turn], TMP[:, 4 * (1 - turn) + j, :], ONES[:, 0:1], j == 0, j == 3)
                mm.then_inc(on_ssq, 1)

            def out_spread(turn):
                pe.wait_ge(on_rs, turn + 1)
                spread(ON_SPREAD[turn], RSTD, 0).then_inc(on_spread, 1)

            pe.wait_ge(v_x, 2)
            out_norm(0)
            pe.wait_ge(gn_n, 4)
            pe.wait_ge(v_b, 2)
            for j in range(4):
                for e in range(2):
                    h = 2 * j + e
                    for c in range(2):
                        mm = pe.matmul(AUX[HD * e:HD * e + HD, j, c * P:(c + 1) * P], VN[:, c, HD * h:HD * h + HD], WT[:, h, :],
                                       start=True, stop=True, skip_group_check=True)
                if j % 2 == 1:
                    mm.then_inc(sp_done, 1)
                if j == 1:
                    out_spread(0)
            base = U0["w_out"]
            sets = [[(n, n * P) for n in range(4)], [(4 + n, n * P) for n in range(4)]]
            pe.wait_ge(xin_ready, KT * 7 + 4)
            unit(base, 0, 0, sets[0], range(4, 8), operand, True, False)
            out_norm(1)
            pe.wait_ge(ug_ready, 4)
            unit(base, 1, 0, sets[1], range(4, 8), operand, True, False, between=[lambda: out_spread(1), lambda: None, lambda: None])
            pe.wait_ge(xin_ready, KT * 8)
            unit(base, 2, 0, sets[0], range(0, 4), operand, False, True)
            unit(base, 3, 0, sets[1], range(0, 4), operand, False, True, between=early_means(5))
            feed_forward(2)

            norm(6, 4)
            for m in range(2):
                for j in range(KT):
                    if m == 0:
                        pe.wait_ge(xo_ready, j + 1)
                    mm = pe.transpose(M[:, 4 * m + j // 2, (j % 2) * P:(j % 2) * P + P], XO[:, j, m * P:(m + 1) * P], IDENT)
                    if j % 4 == 3:
                        mm.then_inc(o_turned, 1)


_INS = ["x", "c", "positions", "ada_w", "ada_b", "norm1_g", "norm2_g", "wqkv_a", "q_norm_a", "k_norm_a",
        "sinks_a", "wo_a", "wqkv_b", "wo_b", "w_gate", "w_up", "w_down", "c_2", "ada_w_2", "ada_b_2",
        "norm1_g_2", "w_in_2", "b_in_2", "a_ln_g_2", "a_ln_b_2", "a_spatial_w_2", "a_spatial_b_2",
        "b_conv_w_2", "b_conv_b_2", "b_gn_g_2", "b_gn_b_2", "out_norm_a_g_2", "out_norm_b_g_2", "w_out_2",
        "norm2_g_2", "w_ffn_in_2", "w_ffn_out_2", "ada_f_w_2", "ada_f_b_2", "norm_f_g_2"]
_SHORT = {"ada_f_w_2": "ada_f_w", "ada_f_b_2": "ada_f_b", "norm_f_g_2": "norm_f_g"}


def kernel(**inputs):
    import concourse.bacc as bacc
    from concourse.bass_utils import run_bass_kernel_spmd

    nc = bacc.Bacc("TRN2", target_bir_lowering=False, num_devices=1)
    arrays, aps = {}, {}
    kept, temp, tril = constants()
    given = {_SHORT.get(n, n): np.ascontiguousarray(inputs[n]) for n in _INS}
    for name, array in {**given, "kept": kept, "temp": temp, "tril": tril}.items():
        arrays[f"in_{name}"] = array
        aps[name] = nc.dram_tensor(f"in_{name}", array.shape, mybir.dt.from_np(array.dtype), kind="ExternalInput").ap()
    out = nc.dram_tensor("out", (1, T, D), F32, kind="ExternalOutput").ap()
    build(nc, aps, out)
    r = run_bass_kernel_spmd(nc, [arrays], core_ids=[0])
    return r.results[0]["out"]
```
